# Optimizing a Trainium2 kernel written in Bass

```python
import math
import jax
import jax.numpy as jnp
from jax import lax
import numpy as np

D_MODEL = 1024
BATCH = 1
SEQ = 256
DEPTH = 2

GRID_W = 64
CTX_LEN = 256
N_MOD = 6
NORM_EPS = 1e-6
NEG_INF = -1e30
ROPE_BASE = 10000.0
Q_BLOCK = 128
A_HEAD_DIM = 64
A_HEADS = D_MODEL // (2 * A_HEAD_DIM)
A_WIDTH = A_HEADS * A_HEAD_DIM
WIN_ROWS_MAX = 8
WIN_COLS = 16
B_WIDTH = D_MODEL // 2
B_CONV = 31
C_WIDTH = D_MODEL // 2
C_CONV = 3
D_QK_DIM = 64
D_V_DIM = 2 * D_QK_DIM
D_HEADS = D_MODEL // (4 * D_QK_DIM)
D_QK_COLS = D_HEADS * 2 * D_QK_DIM
D_WIDTH = D_HEADS * D_V_DIM
EVEN_IN = 3 * A_WIDTH + 2 * B_WIDTH
EVEN_OUT = A_WIDTH + B_WIDTH
ODD_IN = 3 * C_WIDTH + 2 * D_QK_COLS + D_WIDTH
ODD_OUT = C_WIDTH + D_WIDTH
N_GROUPS = 4
EXPERTS_PER_GROUP = 8
N_EXPERTS = N_GROUPS * EXPERTS_PER_GROUP
TOP_K = 2
D_EXPERT = D_MODEL // 4
N_EVEN = (DEPTH + 1) // 2
N_ODD = DEPTH // 2

kernel_name = "hybrid_natten_conformer_shortconv_diffattn_hmoe_dit"

def rmsnorm(x, g):
    x32 = x.astype(jnp.float32)
    y = x32 * lax.rsqrt(jnp.mean(x32 * x32, axis=-1, keepdims=True) + NORM_EPS)
    return (y * g.astype(jnp.float32)).astype(x.dtype)

def layernorm(x, g, b):
    x32 = x.astype(jnp.float32)
    mu = jnp.mean(x32, axis=-1, keepdims=True)
    var = jnp.mean(jnp.square(x32 - mu), axis=-1, keepdims=True)
    y = (x32 - mu) * lax.rsqrt(var + NORM_EPS) * g.astype(jnp.float32) + b.astype(jnp.float32)
    return y.astype(x.dtype)

def depthwise_conv(x, w):
    k, ch = w.shape
    pad = k // 2
    return lax.conv_general_dilated(
        x, w[:, None, :].astype(x.dtype), window_strides=(1,), padding=[(pad, pad)],
        dimension_numbers=('NWC', 'WIO', 'NWC'), feature_group_count=ch)

def axial_rope_tables(n_tok):
    quarter = D_QK_DIM // 4
    t = jnp.arange(n_tok, dtype=jnp.int32)
    row = (t // GRID_W).astype(jnp.float32)
    col = (t % GRID_W).astype(jnp.float32)
    inv = jnp.power(ROPE_BASE, -jnp.arange(quarter, dtype=jnp.float32) / quarter)
    ang = jnp.concatenate([row[:, None] * inv, col[:, None] * inv], axis=-1)
    return jnp.cos(ang), jnp.sin(ang)

def apply_axial_rope(x, cos, sin):
    quarter = x.shape[-1] // 4
    x32 = x.astype(jnp.float32)
    cos = cos[:, None, None, :]
    sin = sin[:, None, None, :]
    parts = []
    for axis in range(2):
        seg = x32[..., 2 * axis * quarter:(2 * axis + 2) * quarter]
        x1, x2 = seg[..., :quarter], seg[..., quarter:]
        ca = cos[..., axis * quarter:(axis + 1) * quarter]
        sa = sin[..., axis * quarter:(axis + 1) * quarter]
        parts += [x1 * ca - x2 * sa, x2 * ca + x1 * sa]
    return jnp.concatenate(parts, axis=-1).astype(x.dtype)

def context_attention(q, k, v):
    s = jnp.einsum('bqhd,bkhd->bhqk', q, k).astype(jnp.float32)
    p = jax.nn.softmax(s, axis=-1).astype(v.dtype)
    return jnp.einsum('bhqk,bkhd->bqhd', p, v)

def neighbourhood_attention(q, k, v, kc, vc, rpb):
    bsz, n_tok, heads, hd = q.shape
    rows = n_tok // GRID_W
    win_r = min(WIN_ROWS_MAX, rows)
    qg = (q * hd ** -0.5).reshape(bsz, rows, GRID_W, heads, hd)
    kg = k.reshape(bsz, rows, GRID_W, heads, hd)
    vg = v.reshape(bsz, rows, GRID_W, heads, hd)
    col = np.arange(GRID_W)
    c_start = np.clip(col - WIN_COLS // 2, 0, GRID_W - WIN_COLS)
    col_ok = (col[None, :] >= c_start[:, None]) & (col[None, :] < c_start[:, None] + WIN_COLS)
    dc = np.clip(col[None, :] - col[:, None], -(WIN_COLS - 1), WIN_COLS - 1) + WIN_COLS - 1

    def one_row(r):
        r_start = jnp.clip(r - win_r // 2, 0, rows - win_r)
        q_r = lax.dynamic_index_in_dim(qg, r, axis=1, keepdims=False)
        k_b = lax.dynamic_slice_in_dim(kg, r_start, win_r, axis=1)
        v_b = lax.dynamic_slice_in_dim(vg, r_start, win_r, axis=1)
        dr = r_start + jnp.arange(win_r) - r + WIN_ROWS_MAX - 1
        bias = rpb[:, dr[:, None, None], dc[None, :, :]]
        s_loc = jnp.einsum('bqhd,bwkhd->bhqwk', q_r, k_b).astype(jnp.float32)
        s_loc = s_loc + bias.transpose(0, 2, 1, 3)[None].astype(jnp.float32)
        s_loc = jnp.where(col_ok[None, None, :, None, :], s_loc, NEG_INF)
        s_ctx = jnp.einsum('bqhd,bchd->bhqc', q_r, kc).astype(jnp.float32)
        s = jnp.concatenate([s_loc.reshape(bsz, heads, GRID_W, win_r * GRID_W), s_ctx], axis=-1)
        p = jax.nn.softmax(s, axis=-1).astype(v.dtype)
        p_loc = p[..., :win_r * GRID_W].reshape(bsz, heads, GRID_W, win_r, GRID_W)
        return (jnp.einsum('bhqwk,bwkhd->bqhd', p_loc, v_b)
                + jnp.einsum('bhqc,bchd->bqhd', p[..., win_r * GRID_W:], vc))

    out = lax.map(one_row, jnp.arange(rows))
    return out.transpose(1, 0, 2, 3, 4).reshape(bsz, n_tok, heads * hd)

def diff_weights(s, lam):
    p = jax.nn.softmax(s, axis=-1)
    return p[:, :, 0] - lam * p[:, :, 1]

def diff_latent_attention(q, k, v, kc, vc, lam):
    bsz, n_tok, heads, _, hd = q.shape
    nb = n_tok // Q_BLOCK
    qb = q.reshape(bsz, nb, Q_BLOCK, heads, 2, hd).transpose(1, 0, 2, 3, 4, 5)

    def block(q_blk):
        s = jnp.concatenate([jnp.einsum('bqhmd,bkhmd->bhmqk', q_blk, k).astype(jnp.float32),
                             jnp.einsum('bqhmd,bchmd->bhmqc', q_blk, kc).astype(jnp.float32)], axis=-1)
        w = diff_weights(s, lam).astype(v.dtype)
        return (jnp.einsum('bhqk,bkhd->bqhd', w[..., :n_tok], v)
                + jnp.einsum('bhqc,bchd->bqhd', w[..., n_tok:], vc))

    out = lax.map(block, qb)
    return out.transpose(1, 0, 2, 3, 4).reshape(bsz, n_tok, heads, D_V_DIM)

def diff_context_attention(q, k, v, lam):
    s = jnp.einsum('bqhmd,bkhmd->bhmqk', q, k).astype(jnp.float32)
    w = diff_weights(s, lam).astype(v.dtype)
    return jnp.einsum('bhqk,bkhd->bqhd', w, v)

def even_mixer(hx, hc, w_in, w_out, rpb, dw, dw_b, ln_g, ln_b, ctx_out):
    def heads(t):
        return t.reshape(t.shape[0], t.shape[1], A_HEADS, A_HEAD_DIM)

    def conformer_conv(u):
        y = depthwise_conv(u, dw) + dw_b
        return jax.nn.silu(layernorm(y, ln_g, ln_b))

    px = hx @ w_in
    qx, kx, vx, ux, gx = jnp.split(px, [A_WIDTH, 2 * A_WIDTH, 3 * A_WIDTH, 3 * A_WIDTH + B_WIDTH], axis=-1)
    if ctx_out:
        pc = hc @ w_in
        qc, kc, vc, uc, gc = jnp.split(pc, [A_WIDTH, 2 * A_WIDTH, 3 * A_WIDTH, 3 * A_WIDTH + B_WIDTH], axis=-1)
    else:
        kc, vc = jnp.split(hc @ w_in[:, A_WIDTH:3 * A_WIDTH], 2, axis=-1)
    kc, vc = heads(kc), heads(vc)
    a_x = neighbourhood_attention(heads(qx), heads(kx), heads(vx), kc, vc, rpb)
    b_x = conformer_conv(ux * jax.nn.sigmoid(gx))
    y_x = jnp.concatenate([a_x, b_x], axis=-1) @ w_out
    if not ctx_out:
        return y_x, None
    a_c = context_attention(heads(qc) * A_HEAD_DIM ** -0.5, kc, vc).reshape(hc.shape[0], hc.shape[1], A_WIDTH)
    b_c = conformer_conv(uc * jax.nn.sigmoid(gc))
    y_c = jnp.concatenate([a_c, b_c], axis=-1) @ w_out
    return y_x, y_c

def odd_mixer(hx, hc, w_in, w_out, conv_w, lam_p, subln_g, lam_init, cos, sin, ctx_out):
    lam_p32 = lam_p.astype(jnp.float32)
    lam = (jnp.exp(jnp.sum(lam_p32[0] * lam_p32[1])) - jnp.exp(jnp.sum(lam_p32[2] * lam_p32[3]))
           + lam_init)
    scale = D_QK_DIM ** -0.5

    def qk_heads(t):
        return t.reshape(t.shape[0], t.shape[1], D_HEADS, 2, D_QK_DIM)

    def v_heads(t):
        return t.reshape(t.shape[0], t.shape[1], D_HEADS, D_V_DIM)

    def short_conv(b_gate, c_gate, u):
        return b_gate * depthwise_conv(c_gate * u, conv_w)

    def diff_out(o):
        return (rmsnorm(o, subln_g) * (1.0 - lam_init)).reshape(o.shape[0], o.shape[1], D_WIDTH)

    cuts = [C_WIDTH, 2 * C_WIDTH, 3 * C_WIDTH, 3 * C_WIDTH + D_QK_COLS, 3 * C_WIDTH + 2 * D_QK_COLS]
    cbx, ccx, cux, dqx, dkx, dvx = jnp.split(hx @ w_in, cuts, axis=-1)
    if ctx_out:
        cbc, ccc, cuc, dqc, dkc, dvc = jnp.split(hc @ w_in, cuts, axis=-1)
    else:
        dkc, dvc = jnp.split(hc @ w_in[:, 3 * C_WIDTH + D_QK_COLS:], [D_QK_COLS], axis=-1)
    kc, vc = qk_heads(dkc), v_heads(dvc)
    qx = apply_axial_rope(qk_heads(dqx) * scale, cos, sin)
    kx = apply_axial_rope(qk_heads(dkx), cos, sin)
    d_x = diff_out(diff_latent_attention(qx, kx, v_heads(dvx), kc, vc, lam))
    y_x = jnp.concatenate([short_conv(cbx, ccx, cux), d_x], axis=-1) @ w_out
    if not ctx_out:
        return y_x, None
    d_c = diff_out(diff_context_attention(qk_heads(dqc) * scale, kc, vc, lam))
    y_c = jnp.concatenate([short_conv(cbc, ccc, cuc), d_c], axis=-1) @ w_out
    return y_x, y_c

def hierarchical_moe(t, wg, bg, we, be, w1, w3, w2):
    n = t.shape[0]
    g_logit = (t @ wg + bg).astype(jnp.float32)
    g_prob = jax.nn.softmax(g_logit, axis=-1)
    g_sel = jnp.argmax(g_logit, axis=-1)
    g_w = jnp.take_along_axis(g_prob, g_sel[:, None], axis=-1)
    e_logit = (t @ we + be).astype(jnp.float32).reshape(n, N_GROUPS, EXPERTS_PER_GROUP)
    e_logit = jnp.take_along_axis(e_logit, g_sel[:, None, None], axis=1)[:, 0]
    top_p, top_i = lax.top_k(jax.nn.softmax(e_logit, axis=-1), TOP_K)
    top_w = top_p / jnp.sum(top_p, axis=-1, keepdims=True) * g_w
    expert_id = g_sel[:, None] * EXPERTS_PER_GROUP + top_i
    combine = jnp.sum(jax.nn.one_hot(expert_id, N_EXPERTS, dtype=jnp.float32) * top_w[..., None], axis=1)

    def add_expert(acc, p):
        w1_e, w3_e, w2_e, c_e = p
        hidden = jax.nn.silu(t @ w1_e) * (t @ w3_e)
        return acc + c_e[:, None] * (hidden @ w2_e), None

    y, _ = lax.scan(add_expert, jnp.zeros_like(t), (w1, w3, w2, combine.T.astype(t.dtype)))
    return y

def setup_inputs(seed: int = 0) -> dict:
    key = jax.random.key(seed)
    ks = iter(jax.random.split(key, 32))

    def nrm(shape, scale):
        return jax.random.normal(next(ks), shape, jnp.float32) * scale

    return {
        "x": nrm((BATCH, SEQ, D_MODEL), 1.0),
        "c": nrm((BATCH, D_MODEL), 1.0),
        "ctx": nrm((BATCH, CTX_LEN, D_MODEL), 1.0),
        "c_ctx": nrm((D_MODEL,), 1.0),
        "w_mod": nrm((DEPTH, D_MODEL, N_MOD * D_MODEL), D_MODEL ** -0.5),
        "b_mod": nrm((DEPTH, N_MOD * D_MODEL), 0.02),
        "norm_mix": 1.0 + nrm((DEPTH, D_MODEL), 0.05),
        "norm_ffn": 1.0 + nrm((DEPTH, D_MODEL), 0.05),
        "norm_final": 1.0 + nrm((D_MODEL,), 0.05),
        "even_w_in": nrm((N_EVEN, D_MODEL, EVEN_IN), D_MODEL ** -0.5),
        "even_w_out": nrm((N_EVEN, EVEN_OUT, D_MODEL), EVEN_OUT ** -0.5),
        "even_rpb": nrm((N_EVEN, A_HEADS, 2 * WIN_ROWS_MAX - 1, 2 * WIN_COLS - 1), 0.02),
        "even_dw": nrm((N_EVEN, B_CONV, B_WIDTH), B_CONV ** -0.5),
        "even_dw_b": nrm((N_EVEN, B_WIDTH), 0.01),
        "even_ln_g": 1.0 + nrm((N_EVEN, B_WIDTH), 0.05),
        "even_ln_b": nrm((N_EVEN, B_WIDTH), 0.01),
        "odd_w_in": nrm((N_ODD, D_MODEL, ODD_IN), D_MODEL ** -0.5),
        "odd_w_out": nrm((N_ODD, ODD_OUT, D_MODEL), ODD_OUT ** -0.5),
        "odd_conv": nrm((N_ODD, C_CONV, C_WIDTH), C_CONV ** -0.5),
        "odd_lambda": nrm((N_ODD, 4, D_QK_DIM), 0.1),
        "odd_subln": 1.0 + nrm((N_ODD, D_V_DIM), 0.05),
        "moe_wg": nrm((DEPTH, D_MODEL, N_GROUPS), D_MODEL ** -0.5),
        "moe_bg": nrm((DEPTH, N_GROUPS), 0.01),
        "moe_we": nrm((DEPTH, D_MODEL, N_EXPERTS), D_MODEL ** -0.5),
        "moe_be": nrm((DEPTH, N_EXPERTS), 0.01),
        "moe_w1": nrm((DEPTH, N_EXPERTS, D_MODEL, D_EXPERT), D_MODEL ** -0.5),
        "moe_w3": nrm((DEPTH, N_EXPERTS, D_MODEL, D_EXPERT), D_MODEL ** -0.5),
        "moe_w2": nrm((DEPTH, N_EXPERTS, D_EXPERT, D_MODEL), D_EXPERT ** -0.5),
    }

def reference(x, c, ctx, c_ctx, w_mod, b_mod, norm_mix, norm_ffn, norm_final,
              even_w_in, even_w_out, even_rpb, even_dw, even_dw_b, even_ln_g, even_ln_b,
              odd_w_in, odd_w_out, odd_conv, odd_lambda, odd_subln,
              moe_wg, moe_bg, moe_we, moe_be, moe_w1, moe_w3, moe_w2):
    bsz, n_tok, d = x.shape
    n_lat = bsz * n_tok
    cos, sin = axial_rope_tables(n_tok)
    silu_c = jax.nn.silu(c)
    silu_cc = jax.nn.silu(c_ctx)
    for l in range(DEPTH):
        ctx_out = l < DEPTH - 1
        mx = jnp.split((silu_c @ w_mod[l] + b_mod[l])[:, None, :], N_MOD, axis=-1)
        mc = jnp.split(silu_cc @ w_mod[l] + b_mod[l], N_MOD, axis=-1)
        hx = rmsnorm(x, norm_mix[l]) * (1.0 + mx[1]) + mx[0]
        hc = rmsnorm(ctx, norm_mix[l]) * (1.0 + mc[1]) + mc[0]
        if l % 2 == 0:
            e = l // 2
            y_x, y_c = even_mixer(hx, hc, even_w_in[e], even_w_out[e], even_rpb[e], even_dw[e],
                                  even_dw_b[e], even_ln_g[e], even_ln_b[e], ctx_out)
        else:
            o = l // 2
            lam_init = 0.8 - 0.6 * math.exp(-0.3 * l)
            y_x, y_c = odd_mixer(hx, hc, odd_w_in[o], odd_w_out[o], odd_conv[o], odd_lambda[o],
                                 odd_subln[o], lam_init, cos, sin, ctx_out)
        x = x + mx[2] * y_x
        hx = rmsnorm(x, norm_ffn[l]) * (1.0 + mx[4]) + mx[3]
        moe_p = (moe_wg[l], moe_bg[l], moe_we[l], moe_be[l], moe_w1[l], moe_w3[l], moe_w2[l])
        if ctx_out:
            ctx = ctx + mc[2] * y_c
            hc = rmsnorm(ctx, norm_ffn[l]) * (1.0 + mc[4]) + mc[3]
            tokens = jnp.concatenate([hx.reshape(-1, d), hc.reshape(-1, d)], axis=0)
            y = hierarchical_moe(tokens, *moe_p)
            x = x + mx[5] * y[:n_lat].reshape(x.shape)
            ctx = ctx + mc[5] * y[n_lat:].reshape(ctx.shape)
        else:
            x = x + mx[5] * hierarchical_moe(hx.reshape(-1, d), *moe_p).reshape(x.shape)
    return rmsnorm(x, norm_final)


_drawn_inputs = setup_inputs


def setup_inputs(seed=0):
    import zlib

    import numpy as np

    out = dict(_drawn_inputs(seed))
    spreads = {}
    factors = {'even_rpb': 3.094, 'odd_subln': 2.754}
    for name, (base, spread) in spreads.items():
        noise = np.random.default_rng([zlib.crc32(name.encode()), seed]).standard_normal(out[name].shape)
        drawn = base * np.exp(spread * noise) if base else spread * noise
        out[name] = jnp.asarray(drawn.astype(out[name].dtype))
    for name, factor in factors.items():
        out[name] = (out[name] * factor).astype(out[name].dtype)
    return out
```

```python
from contextlib import ExitStack

import numpy as np

import concourse.bass as bass
from concourse import mybir

F32 = mybir.dt.float32
I32 = mybir.dt.int32
ALU = mybir.AluOpType
ACT = mybir.ActivationFunctionType
AX = mybir.AxisListType

P = 128
D = 1024
SEQ = 256
CTX = 256
TOK = SEQ + CTX
NCH = D // P
GRID_W = 64
WIN_COLS = 16
EPS = 1e-6
NEG = -1e30
A_HEADS = 8
A_DIM = 64
TAPS = 31
PAD = TAPS // 2
D_HEADS = 4
LAM_INIT = 0.8 - 0.6 * float(np.exp(-0.3))
GROUPS = 4
PER_GROUP = 8
EXPERTS = GROUPS * PER_GROUP
BLK = 256
RING = 12
SLOT = NCH * BLK
PER_LOOP = 4
CAP = 64
NBLK = TOK // CAP
SKIP = 1 << 20
MOD_PER_LAYER = 6
BANKS = 8

C_ID, C_SWAP, C_TRI, C_ONE, C_REV, C_IOTA, C_VAL, C_POW = 0, 128, 256, 384, 512, 640, 672, 688
C_END = 720
LATENT, CONTEXT = 0, 1


def constants():
    c = np.zeros((P, C_END), np.float32)
    i = np.arange(P)
    c[i, C_ID + i] = 1.0
    c[i ^ 16, C_SWAP + i] = 1.0
    c[:, C_TRI:C_TRI + P] = i[:, None] < i[None, :]
    c[:, C_ONE:C_ONE + P] = 1.0
    c[i ^ 63, C_REV + i] = 1.0
    c[:, C_IOTA:C_IOTA + EXPERTS] = np.arange(EXPERTS)
    tok = np.arange(4)[None, :] * P + i[:, None]
    val = np.zeros((P, 4, 2, 2), np.float32)
    for k in (0, 1):
        val[:, :, k, 0] = 2 * tok
        val[:, :, k, 1] = 2 * (2 * tok + k)
    c[:, C_VAL:C_VAL + 16] = val.reshape(P, 16)
    c[:, C_POW:C_POW + EXPERTS] = 8.0 ** (np.arange(EXPERTS) % PER_LOOP)
    quarter = 16
    inv = np.power(np.float32(10000.0), -np.arange(quarter, dtype=np.float32) / quarter).astype(np.float32)
    t = np.arange(SEQ)
    place = np.stack([t // GRID_W, t % GRID_W]).astype(np.float32)
    axis, half, f = (i % 64) // 32, (i % 32) // 16, i % 16
    ang = (place[axis] * inv[f][:, None]).astype(np.float32)
    rot = np.concatenate([np.cos(ang), np.sin(ang) * np.where(half == 0, -1.0, 1.0)[:, None]], 1)
    return c, rot.astype(np.float32)


def psum_plan():
    jobs = []

    def add(name, who):
        jobs.append((name, who))

    def row_vectors(k, what, who):
        for s in (LATENT, CONTEXT):
            for hf in (0, 1):
                add(("row", k, what, s, hf), who)

    def transposed(k, tiles):
        for t in range(tiles):
            for a in (0, 1):
                add(("hT", k, t, a), "act" if a else "dve")

    add(("chan",), "dve")
    add(("mod", 0, 0), "dve")
    add(("mod", 0, 1), "dve")
    row_vectors(0, "scale", "dve")
    row_vectors(0, "shift", "act")
    transposed(0, 4)
    for b in (0, 1):
        for what in ("u", "g"):
            for ft in (0, 1):
                add((what, b, ft), "act")
    for what in ("q", "k"):
        for b in (0, 1):
            for ft in (0, 1):
                add((what, b, ft), "act")
    for b in (0, 1):
        for tp in (0, 1):
            add(("v", b, tp), "act")
    units = 4 * A_HEADS
    add(("S", 0), "act")
    add(("S", 1), "act")
    for n in range(units):
        add(("PT", n), "act")
        if n + 2 < units:
            add(("S", n + 2), "act")
        if n % 4 == 3:
            add(("O", n // 4), "act")
            if 2 + n // 4 < MOD_PER_LAYER:
                add(("mod", 0, 2 + n // 4), "dve")
    add(("mean",), "dve")
    add(("var",), "act")
    row_vectors(0, "gate", "act")
    for b in range(4):
        for tp in (0, 1):
            add(("out", 0, b, tp), "dve")
    row_vectors(1, "scale", "dve")
    row_vectors(1, "shift", "act")
    transposed(1, 4)
    add(("logit", 0), "dve")
    row_vectors(1, "gate", "act")
    add(("rank", 0), "dve")
    for v in range(MOD_PER_LAYER):
        add(("mod", 1, v), "dve")

    row_vectors(2, "scale", "dve")
    row_vectors(2, "shift", "act")
    transposed(2, 4)
    for what in ("dq", "dk"):
        for b in (0, 1):
            for ft in (0, 1):
                add((what, b, ft), "act")
                add((what + "swap", b, ft), "dve")
    for b in (0, 1):
        for tp in (0, 1):
            add(("dv", b, tp), "act")
    for b in (0, 1):
        add(("cc", b), "act")
        add(("cu", b), "dve")
        add(("cb", b), "dve")
    for m in (0, 1):
        add(("DS", 0, m), "act")
    for n in range(2 * D_HEADS):
        if n + 1 < 2 * D_HEADS:
            for m in (0, 1):
                add(("DS", n + 1, m), "act")
        add(("DPT", n), "act")
        add(("DO", n), "dve")
    for n in range(2 * D_HEADS):
        add(("DT", n), "act")
    for s in (LATENT,):
        for hf in (0, 1):
            add(("row", 2, "gate", s, hf), "act")
    for b in range(4):
        add(("out", 1, b, 0), "dve")
    for what, who in (("scale", "dve"), ("shift", "act")):
        for hf in (0, 1):
            add(("row", 3, what, LATENT, hf), who)
    transposed(3, 2)
    add(("logit", 1), "dve")
    for hf in (0, 1):
        add(("row", 3, "gate", LATENT, hf), "act")
    add(("rank", 1), "dve")

    plan, drained, last_of_bank = {}, {"act": 0, "dve": 0}, {}
    for n, (name, who) in enumerate(jobs):
        drained[who] += 1
        plan[name] = dict(n=n, bank=n % BANKS, full=n + 1, who=who, drained=drained[who],
                          before=last_of_bank.get(n % BANKS))
        last_of_bank[n % BANKS] = name
    return plan


def slots_before():
    at, n = {}, 0
    for name, slots in (("mod0a", 8), ("in0", 10), ("mod0b", 16), ("out0", 4), ("mod1", 24),
                        ("moe0", 3 * EXPERTS), ("in1", 12), ("out1", 4), ("moe1", 3 * EXPERTS)):
        at[name] = n
        n += slots
    return at


EVEN_BLOCKS = [("u", 0, 6), ("g", 0, 8), ("u", 1, 7), ("g", 1, 9), ("q", 0, 0), ("q", 1, 1),
               ("k", 0, 2), ("k", 1, 3), ("v", 0, 4), ("v", 1, 5)]
ODD_BLOCKS = [("dq", 0, 6), ("dq", 1, 7), ("dk", 0, 8), ("dk", 1, 9), ("dv", 0, 10), ("dv", 1, 11),
              ("cc", 0, 2), ("cu", 0, 4), ("cb", 0, 0), ("cc", 1, 3), ("cu", 1, 5), ("cb", 1, 1)]


def trunk(nc, A):
    plan = psum_plan()
    at = slots_before()

    ctx = ExitStack()
    with ctx:
        def sb(name, shape, dt=F32):
            return ctx.enter_context(nc.sbuf_tensor(name, shape, dt))

        def sem(name):
            return ctx.enter_context(nc.semaphore(name))

        X = sb("X", [P, 4, D])
        ring = sb("ring", [P, RING, SLOT])
        RH = sb("RH", [P, 4096])
        RT = sb("RT", [P, 4096])
        RAB = sb("RAB", [P, 4096])
        G = sb("G", [P, 2, D])
        modrow = sb("modrow", [P, MOD_PER_LAYER, BLK])
        grow = sb("grow", [P, 2, BLK])
        const = sb("const", [P, C_END])
        csilu = sb("csilu", [P, NCH, 32])
        craw = sb("craw", [P, 2, NCH])
        WR = sb("WR", [P, NCH, GROUPS + EXPERTS])
        RB = sb("RB", [P, GROUPS + EXPERTS])
        RM = sb("RM", [P, 2288])
        BIAS = sb("BIAS", [P, 4, 6, 64])
        PR = sb("PR", [P, 2, 512])
        diag = sb("diag", [P, 4, P])
        chan = sb("chan", [P, 4, 40])
        small = sb("small", [P, 256])
        idx = sb("idx", [P, NBLK, EXPERTS, 2], I32)
        sidx = sb("sidx_all", [P, 24], I32)
        val_i = sb("val_i", [P, 4, 2, 2], I32)
        pos_i = sb("pos_i", [P, 2, 4, 2], I32)
        extra_i = sb("extra_i", [1, 2, EXPERTS // PER_LOOP], I32)
        skip_i = sb("skip_i", [P, 256], I32)
        ps = ctx.enter_context(nc.psum_tensor("ps", [P, BANKS, 512], F32))

        ident = const[:, C_ID:C_ID + P]
        swap = const[:, C_SWAP:C_SWAP + P]
        tri = const[:, C_TRI:C_TRI + P]
        reverse = const[:, C_REV:C_REV + P]
        ones = const[:, C_ONE:C_ONE + P]
        iota = const[:, C_IOTA:C_IOTA + EXPERTS]

        H = RH[:, :].rearrange("p (t d) -> p t d", t=4)
        QK = RH[:, :].rearrange("p (f t) -> p f t", f=8)
        DQ = RH[:, 0:1024].rearrange("p (f t) -> p f t", f=4)
        DK = RH[:, 1024:3072].rearrange("p (f t) -> p f t", f=4)
        ROT = RH[:, 3072:4096].rearrange("p (b t) -> p b t", b=2)
        hT = RT[:, :].rearrange("p (c t) -> p c t", c=NCH)
        aT = RT[:, 0:2048].rearrange("p (f t) -> p f t", f=4)
        PTX = RT[:, 2048:3072].rearrange("p (k q) -> p k q", k=4)
        PTC = RT[:, 3072:3584].rearrange("p (k q) -> p k q", k=2)
        dT = RT[:, 0:1024].rearrange("p (f t) -> p f t", f=4)
        DPT = RT[:, 2048:3072].rearrange("p (b k q) -> p b k q", b=2, k=4)
        GF = modrow[:, 0:4, :].rearrange("p v n -> p (v n)")
        chan_rows = PR[:, 0, :]
        LAMROW = PR[:, 0, 0:256]
        SCALE = RAB[:, 0:2048].rearrange("p (s d) -> p s d", s=2)
        SHIFT = RAB[:, 2048:4096].rearrange("p (s d) -> p s d", s=2)
        V = RAB[:, 0:2048].rearrange("p (t d) -> p t d", t=4)
        Y = RAB[:, 2048:4096].rearrange("p (c t) -> p c t", c=4)
        DP = RAB[:, 2048:4096].rearrange("p (n k) -> p n k", n=4)
        YP = RAB[:, :].rearrange("p (b k d) -> p b k d", b=2, k=2)
        Z = RM[:, :].rearrange("p (c s t) -> p c s t", c=4, s=2)
        SQ = RM[:, 0:2048].rearrange("p (c t) -> p c t", c=4)
        SG = PR
        SD = PR[:, 0, :]
        CU = RM[:, 0:4 * (SEQ + 2)].rearrange("p (c t) -> p c t", c=4)
        CC = RM[:, 1032:1032 + 1024].rearrange("p (c t) -> p c t", c=4)
        BIASF = BIAS[:, :, :, :].rearrange("p h j k -> p (h j k)")
        COS, SIN = BIASF[:, 0:SEQ], BIASF[:, SEQ:2 * SEQ]
        CV = BIASF[:, 512:1536].rearrange("p (c t) -> p c t", c=4)
        OD = PR[:, :, :].rearrange("p a b -> p (a b)").rearrange("p (n d) -> p n d", n=8)
        XG = RH[:, 0:2048].rearrange("p (b d) -> p b d", b=4)
        YS = RH[:, 2048:3072].rearrange("p (b d) -> p b d", b=2)
        XGX, YSX = RH[:, 3072:3584], RH[:, 3584:4096]
        XT = RT[:, 0:1024].rearrange("p (b j a s) -> p b j a s", b=2, j=4, a=2)
        XTX = RT[:, 1024:1536].rearrange("p (j a s) -> p j a s", j=4, a=2)
        SA = RT[0:CAP, 1536:2048].rearrange("p (b f) -> p b f", b=2)
        HID = RT[0:CAP, 2048:2560].rearrange("p (b f) -> p b f", b=2)
        SAX, HIDX = RT[0:CAP, 2560:2816], RT[0:CAP, 2816:3072]
        HT = RT[:, 3072:3328].rearrange("p (b f s) -> p b f s", b=2, f=2)
        HTX = RT[:, 3328:3456].rearrange("p (f s) -> p f s", f=2)
        GIDX = [sidx[:, 2 * b:2 * b + 1] for b in range(4)]
        SIDX = [sidx[:, 8 + 2 * b:9 + 2 * b] for b in range(2)]
        GIDXX, SIDXX = sidx[:, 12:13], sidx[:, 14:15]

        sumsq = small[:, 0:20].rearrange("p (k t) -> p k t", k=5)
        root = small[:, 20:40].rearrange("p (k t) -> p k t", k=5)
        rstd = small[:, 40:60].rearrange("p (k t) -> p k t", k=5)
        eps = small[:, 60:61]
        nmax = small[:, 64:96]
        m1 = small[:, 96:97]
        m2 = small[:, 97:98]
        sums = small[:, 100:108]
        rsum = small[:, 112:116]
        lam = small[:, 116:124]
        subln = small[:, 124:125]
        sublns = small[:, 125:126]
        dss = small[:, 128:136]
        droot = small[:, 136:144]
        drstd = small[:, 144:152]
        topw = small[:, 152:160].rearrange("p (t k) -> p t k", t=4)
        def temp(at, *shape):
            n = int(np.prod(shape))
            names = "abcd"[:len(shape)]
            return RM[:, at:at + n].rearrange(f"p ({' '.join(names)}) -> p {' '.join(names)}",
                                              **{k: v for k, v in zip(names, shape)})
        logits = temp(0, 4, GROUPS + EXPERTS)
        chosen = temp(144, 4, EXPERTS)
        first_choice, second_choice = temp(272, 4, EXPERTS), temp(400, 4, EXPERTS)
        masked, cand, place = temp(528, 4, EXPERTS), temp(656, 4, EXPERTS), temp(784, 4, EXPERTS)
        gcand, ghot, gpen = temp(912, 4, GROUPS), temp(928, 4, GROUPS), temp(944, 4, GROUPS)
        rarg = temp(960, 5, 4)
        rexp = temp(980, 5, 4)
        gmax, emax, emax2, least, gsum, pos_f = [temp(1000 + 4 * i, 4) for i in range(6)]
        count, blocks, packed = temp(1032, EXPERTS), temp(1064, EXPERTS), temp(1096, EXPERTS)
        words = temp(1128, EXPERTS // PER_LOOP)

        psum_full = sem("psum_full")
        act_drained = sem("act_drained")
        dve_drained = sem("dve_drained")
        landed = [sem(f"landed{i}") for i in range(RING)]
        ring_free = sem("ring_free")
        ld_const, ld_x, ld_c, ld_bmod, ld_rows, ld_grow, ld_router, ld_lam, ld_rot, ld_final = (
            sem(n) for n in ("ld_const", "ld_x", "ld_c", "ld_bmod", "ld_rows", "ld_grow", "ld_router",
                             "ld_lam", "ld_rot", "ld_final"))
        ld_bias = [sem(f"ld_bias{i}") for i in range(4)]
        pe_passed, pool_passed = sem("pe_passed"), sem("pool_passed")
        zeroed = sem("zeroed")
        dve_zeroed = sem("dve_zeroed")
        c_silu = sem("c_silu")
        act_step, dve_step, pool_step = sem("act_step"), sem("dve_step"), sem("pool_step")
        norm_root = sem("norm_root")
        h_scaled = sem("h_scaled")
        h_ready = sem("h_ready")
        row_scale = sem("row_scale")
        gated_in = sem("gated_in")
        z_clear = sem("z_clear")
        conv_step = sem("conv_step")
        bias_ready = sem("bias_ready")
        max_ready = sem("max_ready")
        diag_ready = sem("diag_ready")
        centred = sem("centred")
        squared = sem("squared")
        ln_scaled = sem("ln_scaled")
        b_ready = sem("b_ready")
        x_updated = sem("x_updated")
        h_stored = sem("h_stored")
        router_exp = sem("router_exp")
        router_max = sem("router_max")
        one_hot = sem("one_hot")
        pos_ready = sem("pos_ready")
        table_set = sem("table_set")
        table_written = sem("table_written")
        idx_raw = sem("idx_raw")
        extra_ready = sem("extra_ready")
        gidx_ready, sidx_ready = sem("gidx_ready"), sem("sidx_ready")
        gathered = [sem(f"gathered{i}") for i in range(4)]
        scattered = [sem(f"scattered{i}") for i in range(2)]
        xT_full, xT_ready = sem("xT_full"), sem("xT_ready")
        up_full, gate_ready, hid_ready = sem("up_full"), sem("gate_ready"), sem("hid_ready")
        hidT_full, hidT_ready = sem("hidT_full"), sem("hidT_ready")
        y_full, y_ready = sem("y_full"), sem("y_ready")
        x_gidx, x_gathered, x_scattered = sem("x_gidx"), sem("x_gathered"), sem("x_scattered")
        x_xT_full, x_xT_ready = sem("x_xT_full"), sem("x_xT_ready")
        x_up_full, x_gate_ready, x_hid_ready = sem("x_up_full"), sem("x_gate_ready"), sem("x_hid_ready")
        x_hidT_full, x_hidT_ready = sem("x_hidT_full"), sem("x_hidT_ready")
        x_y_full, x_y_ready = sem("x_y_full"), sem("x_y_ready")
        y_back = [sem(f"y_back{i}") for i in range(2)]
        combined = sem("combined")
        stored = sem("stored")
        lam_sums, lam_exp, lam_ready = sem("lam_sums"), sem("lam_exp"), sem("lam_ready")
        o_squared = sem("o_squared")
        o_root = sem("o_root")
        odiag = sem("odiag")
        final_ready = sem("final_ready")
        rot_ready = sem("rot_ready")

        tiles_of = {0: 4, 1: 2}
        tokens = [P * tiles_of[l] for l in (0, 1)]
        hrow = [nc.dram_tensor(f"hrow{l}", [2 * tokens[l], 512], F32).ap() for l in (0, 1)]
        table = [nc.dram_tensor(f"table{l}", [tokens[l] * EXPERTS, 2], I32).ap() for l in (0, 1)]
        pair_out = [nc.dram_tensor(f"pair_out{l}", [4 * tokens[l], 512], F32).ap() for l in (0, 1)]

        norm_tiles = [4, 4, 4, 2, 2]
        h_before = [sum(norm_tiles[:k]) for k in range(6)]
        xu_mix = [8, 8 + 4 + 4]
        xu_moe = [8 + 4, 8 + 4 + 4 + 2]

        block = ctx.enter_context(nc.Block())

        def full(eng, *name):
            eng.wait_ge(psum_full, plan[name]["full"])
            return ps[:, plan[name]["bank"], :]

        def drained(eng, *name):
            job = plan[name]
            eng.wait_ge(act_drained if job["who"] == "act" else dve_drained, job["drained"])

        def job_after(i, q, k):
            return (i, q + k) if q + k < PER_LOOP else (i + 1, q + k - PER_LOOP)

        def extra_counts(eng, l, i):
            word = eng.value_load(extra_i[0:1, l, i:i + 1] if isinstance(i, int) else
                                  extra_i[0:1, l, bass.ds(i, 1)], min_val=0, max_val=4095)
            return [(word >> (3 * q)) & 7 for q in range(PER_LOOP)]

        def chained(eng, semaphore):
            count = [0]

            def step(ins, wait=True):
                count[0] += 1
                ins.then_inc(semaphore, 1)
                if wait:
                    eng.wait_ge(semaphore, count[0])

            step.sync = lambda: eng.wait_ge(semaphore, count[0])
            step.lag = lambda n: eng.wait_ge(semaphore, count[0] - n)
            return step

        @block.sync
        def _(sp):
            sp.dma_start(const[:, :], A["consts"]).then_inc(ld_const, 16)
            slots_filled = [0]

            def load(halves):
                n = slots_filled[0]
                if n >= RING:
                    sp.wait_ge(ring_free, n - RING + 1)
                for dst, src in halves(ring[:, n % RING, :]):
                    sp.dma_start(dst, src).then_inc(landed[n % RING], 16)
                slots_filled[0] += 1

            def columns(w, b, rows="features"):
                w = w[:, b * BLK:(b + 1) * BLK]

                def halves(slot):
                    for a in (0, 1):
                        rows_a = w[512 * a:512 * (a + 1), :]
                        yield (slot[:, 1024 * a:1024 * (a + 1)].rearrange("p (j n) -> p j n", n=BLK),
                               rows_a.rearrange("(p j) n -> p j n", j=4) if rows == "features" else
                               rows_a.rearrange("(j p) n -> p j n", p=P))

                load(halves)

            def modulation(l, vectors):
                for v in vectors:
                    for b in range(4):
                        columns(A["w_mod"][l], 4 * v + b)

            def experts(l):
                base = at[f"moe{l}"]
                assert slots_filled[0] == base
                with sp.Fori(0, EXPERTS // PER_LOOP) as i:
                    for q in range(PER_LOOP):
                        for k, name in enumerate(("moe_w1", "moe_w3", "moe_w2")):
                            n = base + 3 * q + k
                            sp.wait_ge(ring_free, i * RING + (n - RING + 1))
                            w = A[name][l, bass.ds(i * PER_LOOP + q, 1), :, :]
                            for a in (0, 1):
                                if k < 2:
                                    src = w[:, 512 * a:512 * (a + 1), :].rearrange("e (p j) n -> p (e j n)", j=4)
                                else:
                                    src = w.rearrange("e (p f) n -> p f (e n)", p=P)[:, a, :]
                                sp.dma_start(ring[:, n % RING, 1024 * a:1024 * (a + 1)],
                                             src).then_inc(landed[n % RING], 16)
                slots_filled[0] += 3 * EXPERTS

            sp.dma_start(X[:, 0:2, :], A["x"][0].rearrange("(t p) d -> p t d", p=P)).then_inc(ld_x, 16)
            sp.dma_start(X[:, 2:4, :], A["ctx"][0].rearrange("(t p) d -> p t d", p=P)).then_inc(ld_x, 16)
            modulation(0, (0, 1))
            for _, _, b in EVEN_BLOCKS:
                columns(A["even_w_in"][0], b)
            modulation(0, (2, 3, 4, 5))
            for b in range(4):
                columns(A["even_w_out"][0], b, rows="tiles")
            modulation(1, range(MOD_PER_LAYER))
            experts(0)
            for _, _, b in ODD_BLOCKS:
                columns(A["odd_w_in"][0], b)
            for b in range(4):
                columns(A["odd_w_out"][0], b, rows="tiles")
            experts(1)
            sp.wait_ge(stored, 32)

        @block.tensor
        def _(pe):
            order = iter(plan)
            used = [0]

            def open_bank(*name):
                assert next(order) == name, name
                before = plan[name]["before"]
                if before:
                    drained(pe, *before)
                return ps[:, plan[name]["bank"], :]

            def close(mm):
                mm.then_inc(psum_full, 1)

            free_due = [0]

            def free(k):
                free_due[0] += k

            def freed(mm):
                if free_due[0]:
                    mm.then_inc(ring_free, free_due[0])
                    free_due[0] = 0

            def slot(n):
                pe.wait_ge(landed[n % RING], 32 * (n // RING + 1))
                return ring[:, n % RING, :].rearrange("p (c n) -> p c n", n=BLK)

            def modulation(l, v, first):
                bank = open_bank("mod", l, v)
                pe.wait_ge(c_silu, 1)
                w = [slot(first + j) for j in range(4)]
                for c in range(NCH):
                    for j in range(4):
                        mm = pe.matmul(bank[32 * j:32 * j + 32, 0:BLK], csilu[:, c, :], w[j][:, c, :],
                                       start=(c == 0), stop=(c == NCH - 1))
                        if c == 0 and j == 0:
                            freed(mm)
                close(mm)
                free(4)

            def rows(k, what, v, streams=(LATENT, CONTEXT)):
                for s in streams:
                    for hf in (0, 1):
                        bank = open_bank("row", k, what, s, hf)
                        if what == "scale":
                            pe.wait_ge(row_scale, k + 1)
                        else:
                            drained(pe, "mod", k // 2, v)
                        for j in (2 * hf, 2 * hf + 1):
                            mm = pe.matmul(bank[:, BLK * (j % 2):BLK * (j % 2 + 1)],
                                           ident[:, 32 * j + s:32 * j + s + 1].broadcast_to([P, P]),
                                           modrow[:, v, :], start=True, stop=True)
                            freed(mm)
                        close(mm)

            def transposes(k):
                for t in range(norm_tiles[k]):
                    pe.wait_ge(h_ready, h_before[k] + t + 1)
                    for a in (0, 1):
                        bank = open_bank("hT", k, t, a)
                        for j in range(4):
                            mm = pe.transpose(bank[:, P * j:P * (j + 1)], H[:, t, 512 * a + j:512 * (a + 1):4],
                                              ident)
                            if j == 0:
                                freed(mm)
                        close(mm)

            def by_feature(bank, w, ft, moving):
                for c in range(NCH):
                    mm = pe.matmul(bank, w[:, c, P * ft:P * (ft + 1)], moving[:, c, :],
                                   start=(c == 0), stop=(c == NCH - 1))
                    if c == 0:
                        freed(mm)
                return mm

            def by_token(bank, w, tiles, chunk_of):
                for i, t in enumerate(tiles):
                    for c in range(NCH):
                        mm = pe.matmul(bank[:, BLK * i:BLK * (i + 1)], chunk_of(c, t), w[:, c, :],
                                       start=(c == 0), stop=(c == NCH - 1))
                        if c == 0:
                            freed(mm)
                return mm

            def router(l):
                T = tiles_of[l]
                bank = open_bank("logit", l)
                pe.wait_ge(ld_router, 16 * 6 * (l + 1))
                for t in range(T):
                    for c in range(NCH):
                        mm = pe.matmul(bank[:, 36 * t:36 * t + 36], hT[:, c, P * t:P * (t + 1)], WR[:, c, :],
                                       start=(c == 0), stop=(c == NCH - 1))
                close(mm)

            def ranks(l):
                T = tiles_of[l]
                bank = open_bank("rank", l)
                pe.wait_ge(one_hot, l + 1)
                M = chosen
                for t in range(T):
                    out = bank[:, EXPERTS * t:EXPERTS * (t + 1)]
                    for u in range(t):
                        pe.matmul(out, ones, M[:, u, :], start=(u == 0), stop=False)
                    mm = pe.matmul(out, tri, M[:, t, :], start=(t == 0), stop=True)
                for t in range(T):
                    mm = pe.matmul(bank[:, EXPERTS * 4:EXPERTS * 5], ones, M[:, t, :],
                                   start=(t == 0), stop=(t == T - 1))
                close(mm)

            extras = pe.alloc_register("pe_extras")
            pe.reg_mov(extras, 0)

            def experts(l):
                n0, base = EXPERTS * l, at[f"moe{l}"]
                end = plan[("mod", 1, 5) if l == 0 else ("rank", 1)]["n"]
                for name in list(plan)[end - BANKS + 1:end + 1]:
                    drained(pe, *name)

                def T(i, q, start=False):
                    n, b = i * PER_LOOP + (n0 + q), q % 2
                    pe.wait_ge(gathered[q % 4], (i + ((n0 + q) // 4 + 1)) * 16)
                    if not start:
                        pe.wait_ge(xT_ready, n - 1)
                    for j in range(4):
                        mm = pe.transpose(ps[:, b, P * j:P * (j + 1)], XG[:, q % 4, j:512:4], ident)
                        if j == 0:
                            freed(mm)
                    mm.then_inc(xT_full, 1)

                def wait_slot(i, q, k):
                    s = base + 3 * q + k
                    pe.wait_ge(landed[s % RING], (i + (s // RING + 1)) * 32)
                    return ring[:, s % RING, :]

                def U(i, q, start=False):
                    n, b = i * PER_LOOP + (n0 + q), q % 2
                    pe.wait_ge(xT_ready, n + 1)
                    if not start:
                        pe.wait_ge(hid_ready, n - 1)
                    w = [wait_slot(i, q, k) for k in (0, 1)]
                    up(w, lambda c: XT[:, b, c % 4, c // 4, :], ps[:, 2 + b, :]).then_inc(up_full, 1)

                def up(w, xt, bank):
                    for c in range(NCH):
                        for k in (0, 1):
                            mm = pe.matmul(bank[CAP * k:CAP * (k + 1), 0:BLK], xt(c),
                                           w[k][:, BLK * c:BLK * (c + 1)], start=(c == 0), stop=(c == NCH - 1))
                    return mm

                def Hd(i, q):
                    n, b = i * PER_LOOP + (n0 + q), q % 2
                    pe.wait_ge(hid_ready, n + 1)
                    pe.sem_inc(pe_passed, 1)
                    for f in (0, 1):
                        mm = pe.transpose(ps[:, 4, 128 * b + CAP * f:128 * b + CAP * (f + 1)],
                                          HID[:, b, f:BLK:2], ident[0:CAP, 0:CAP])
                        if f == 0:
                            freed(mm)
                    mm.then_inc(hidT_full, 1)

                def Dn(i, q):
                    n, b = i * PER_LOOP + (n0 + q), q % 2
                    pe.wait_ge(hidT_ready, n + 1)
                    w = wait_slot(i, q, 2)
                    down(w, lambda f: HT[:, b, f, :], ps[:, 5 + b, :]).then_inc(y_full, 1)

                def down(w, ht, bank):
                    for f in (0, 1):
                        for k in (0, 1):
                            mm = pe.matmul(bank[CAP * k:CAP * (k + 1), :], ht(f),
                                           w[:, D * f + 512 * k:D * f + 512 * (k + 1)],
                                           start=(f == 0), stop=(f == 1))
                    return mm

                def more(q, count):
                    w = [ring[:, (base + 3 * q + k) % RING, :] for k in range(3)]
                    bank = ps[:, 7, :]
                    with pe.If(count > 0):
                        with pe.Fori(0, count):
                            pe.wait_ge(x_y_ready, pe.snap(extras))
                            pe.reg_add(extras, extras, 1)
                            x = pe.snap(extras)
                            pe.wait_ge(x_gathered, x * 16)
                            for j in range(4):
                                mm = pe.transpose(bank[:, P * j:P * (j + 1)], XGX[:, j:512:4], ident)
                            mm.then_inc(x_xT_full, 1)
                            pe.wait_ge(x_xT_ready, x)
                            up(w, lambda c: XTX[:, c % 4, c // 4, :], bank).then_inc(x_up_full, 1)
                            pe.wait_ge(x_hid_ready, x)
                            pe.sem_inc(pe_passed, 1)
                            for f in (0, 1):
                                mm = pe.transpose(bank[:, CAP * f:CAP * (f + 1)], HIDX[:, f:BLK:2],
                                                  ident[0:CAP, 0:CAP])
                            mm.then_inc(x_hidT_full, 1)
                            pe.wait_ge(x_hidT_ready, x)
                            down(w[2], lambda f: HTX[:, f, :], bank).then_inc(x_y_full, 1)

                def step(i, q, count, ahead2=True, ahead1=True):
                    if ahead2:
                        T(*job_after(i, q, 2))
                    Hd(i, q)
                    if ahead1:
                        U(*job_after(i, q, 1))
                    Dn(i, q)
                    more(q, count)
                    free(3)

                T(0, 0, start=(l == 0))
                T(0, 1, start=(l == 0))
                U(0, 0, start=(l == 0))
                pe.wait_ge(extra_ready, l + 1)

                last = EXPERTS // PER_LOOP - 1
                c = extra_counts(pe, l, 0)
                for q in range(PER_LOOP):
                    step(0, q, c[q])
                with pe.Fori(1, last) as i:
                    c = extra_counts(pe, l, i)
                    for q in range(PER_LOOP):
                        step(i, q, c[q])
                c = extra_counts(pe, l, last)
                for q in range(PER_LOOP):
                    step(last, q, c[q], ahead2=(q < 2), ahead1=(q < 3))
                pe.wait_ge(y_ready, n0 + EXPERTS)
                pe.wait_ge(x_y_ready, pe.snap(extras))

            pe.wait_ge(ld_const, 16)
            bank = open_bank("chan")
            pe.wait_ge(ld_rows, 16 * 5)
            for c in range(4):
                mm = pe.transpose(bank[:, 40 * c:40 * c + 37], chan_rows[0:37, P * c:P * (c + 1)], ident[0:37, 0:37])
            close(mm)
            n = at["mod0a"]
            modulation(0, 0, n)
            modulation(0, 1, n + 4)
            rows(0, "scale", 1)
            rows(0, "shift", 0)
            transposes(0)
            drained(pe, "hT", 0, 3, 0)
            drained(pe, "hT", 0, 3, 1)
            for i, (what, b, _) in enumerate(EVEN_BLOCKS):
                w = slot(at["in0"] + i)
                if what == "v":
                    for tp in (0, 1):
                        bank = open_bank(what, b, tp)
                        close(by_token(bank, w, (2 * tp, 2 * tp + 1), lambda c, t: hT[:, c, P * t:P * (t + 1)]))
                else:
                    for ft in (0, 1):
                        bank = open_bank(what, b, ft)
                        close(by_feature(bank, w, ft, hT))
                free(1)

            def scores(n):
                h, qt = n // 4, n % 4
                ft, p0 = h // 2, A_DIM * (h % 2)
                bank = open_bank("S", n)
                drained(pe, "q", ft // 2, ft % 2)
                drained(pe, "k", ft // 2, ft % 2)
                k0 = 0 if qt < 2 else SEQ
                mm = pe.matmul(bank[:, k0:TOK], QK[p0:p0 + A_DIM, ft, P * qt:P * (qt + 1)],
                               QK[p0:p0 + A_DIM, 4 + ft, k0:TOK], start=True, stop=(qt >= 2),
                               skip_group_check=(qt < 2))
                if qt < 2:
                    pe.wait_ge(bias_ready, h + 1)
                    start = (2 - 2 * qt) * GRID_W
                    bias = BIAS[:, h % 4, :, :].rearrange("p j k -> p (j k)")[:, start:start + SEQ]
                    mm = pe.matmul(bank[:, 0:SEQ], reverse, bias, start=False, stop=True, skip_group_check=True)
                close(mm)

            def probs_T(n):
                qt = n % 4
                bank = open_bank("PT", n)
                pe.wait_ge(diag_ready, n + 1)
                for kt in range(0 if qt < 2 else 2, 4):
                    mm = pe.matmul(bank[:, P * kt:P * (kt + 1)], PR[:, n % 2, P * kt:P * (kt + 1)],
                                   diag[:, n % 2, :], start=True, stop=True)
                    if kt == 2:
                        freed(mm)
                close(mm)

            def weighted(h):
                p0 = A_DIM * (h % 2)
                bank = open_bank("O", h)
                for n in range(4 * h, 4 * h + 4):
                    drained(pe, "PT", n)
                if h == 0:
                    for tp in (0, 1):
                        drained(pe, "v", 1, tp)
                for kt in range(4):
                    mm = pe.matmul(bank[p0:p0 + A_DIM, 0:SEQ], V[:, kt, A_DIM * h:A_DIM * (h + 1)], PTX[:, kt, :],
                                   start=(kt == 0), stop=(kt == 3))
                for kt in (2, 3):
                    mm = pe.matmul(bank[p0:p0 + A_DIM, SEQ:TOK], V[:, kt, A_DIM * h:A_DIM * (h + 1)],
                                   PTC[:, kt - 2, :], start=(kt == 2), stop=(kt == 3))
                close(mm)

            units = 4 * A_HEADS
            scores(0)
            scores(1)
            for n in range(units):
                probs_T(n)
                if n + 2 < units:
                    scores(n + 2)
                if n % 4 == 3:
                    weighted(n // 4)
                    if 2 + n // 4 < MOD_PER_LAYER:
                        modulation(0, 2 + n // 4, at["mod0b"] + n - 3)

            bank = open_bank("mean")
            pe.wait_ge(conv_step, 4 * TAPS)
            for ct in range(4):
                mm = pe.matmul(bank, ones, Y[:, ct, :], start=(ct == 0), stop=(ct == 3))
            close(mm)
            bank = open_bank("var")
            for ct in range(4):
                pe.wait_ge(squared, ct + 1)
                mm = pe.matmul(bank, ones, SQ[:, ct, :], start=(ct == 0), stop=(ct == 3))
            close(mm)
            rows(0, "gate", 2)
            drained(pe, "O", A_HEADS - 1)
            for b in range(4):
                w = slot(at["out0"] + b)
                for tp in (0, 1):
                    bank = open_bank("out", 0, b, tp)
                    pe.wait_ge(b_ready, 4)
                    close(by_token(bank, w, (2 * tp, 2 * tp + 1),
                                   lambda c, t: (aT if c < 4 else Y)[:, c % 4, P * t:P * (t + 1)]))
                free(1)
            rows(1, "scale", 4)
            rows(1, "shift", 3)
            transposes(1)
            drained(pe, "hT", 1, 3, 0)
            drained(pe, "hT", 1, 3, 1)
            router(0)
            rows(1, "gate", 5)
            ranks(0)
            for v in range(MOD_PER_LAYER):
                modulation(1, v, at["mod1"] + 4 * v)
            experts(0)

            rows(2, "scale", 1)
            rows(2, "shift", 0)
            transposes(2)
            drained(pe, "hT", 2, 3, 0)
            drained(pe, "hT", 2, 3, 1)
            for i, (what, b, _) in enumerate(ODD_BLOCKS):
                w = slot(at["in1"] + i)
                if what == "dv":
                    for tp in (0, 1):
                        bank = open_bank(what, b, tp)
                        close(by_token(bank, w, (2 * tp, 2 * tp + 1), lambda c, t: hT[:, c, P * t:P * (t + 1)]))
                elif what in ("dq", "dk"):
                    tok = SEQ if what == "dq" else TOK
                    for ft in (0, 1):
                        bank = open_bank(what, b, ft)
                        close(by_feature(bank[:, 0:tok], w, ft, hT[:, :, 0:tok]))
                        bank = open_bank(what + "swap", b, ft)
                        drained(pe, what, b, ft)
                        src = (DQ if what == "dq" else DK)[:, 2 * b + ft, 0:SEQ]
                        close(pe.matmul(bank[:, 0:SEQ], swap, src, start=True, stop=True))
                else:
                    bank = open_bank(what, b)
                    for ft in (0, 1):
                        mm = by_feature(bank[:, SEQ * ft:SEQ * (ft + 1)], w, ft, hT[:, :, 0:SEQ])
                    close(mm)
                free(1)

            def diff_scores(n):
                h, qt = n // 2, n % 2
                if qt == 0:
                    pe.wait_ge(rot_ready, 4 + h + 1)
                for m in (0, 1):
                    bank = open_bank("DS", n, m)
                    mm = pe.matmul(bank, DQ[64 * m:64 * m + 64, h, P * qt:P * (qt + 1)],
                                   DK[64 * m:64 * m + 64, h, :], start=True, stop=True)
                    close(mm)

            diff_scores(0)
            for n in range(2 * D_HEADS):
                h, qt = n // 2, n % 2
                if n + 1 < 2 * D_HEADS:
                    diff_scores(n + 1)
                bank = open_bank("DPT", n)
                pe.wait_ge(diag_ready, units + n + 1)
                for kt in range(4):
                    for m in (0, 1):
                        mm = pe.matmul(bank[:, P * kt:P * (kt + 1)], DP[:, 2 * (n % 2) + m, P * kt:P * (kt + 1)],
                                       diag[:, 2 * (n % 2) + m, :], start=(m == 0), stop=(m == 1))
                close(mm)
                bank = open_bank("DO", n)
                drained(pe, "DPT", n)
                if n == 0:
                    drained(pe, "dv", 1, 1)
                for kt in range(4):
                    mm = pe.matmul(bank[:, 0:P], DPT[:, n % 2, kt, :], V[:, kt, P * h:P * (h + 1)],
                                   start=(kt == 0), stop=(kt == 3))
                close(mm)
            for n in range(2 * D_HEADS):
                bank = open_bank("DT", n)
                pe.wait_ge(odiag, n + 1)
                close(pe.matmul(bank[:, 0:P], OD[:, n, :], diag[:, n % 4, :], start=True, stop=True))
            rows(2, "gate", 2, (LATENT,))
            drained(pe, "DT", 2 * D_HEADS - 1)
            drained(pe, "cb", 0)
            drained(pe, "cb", 1)
            for b in range(4):
                w = slot(at["out1"] + b)
                bank = open_bank("out", 1, b, 0)
                close(by_token(bank, w, (0, 1), lambda c, t: (CV if c < 4 else dT)[:, c % 4, P * t:P * (t + 1)]))
                free(1)
            rows(3, "scale", 4, (LATENT,))
            rows(3, "shift", 3, (LATENT,))
            transposes(3)
            drained(pe, "hT", 3, 1, 0)
            drained(pe, "hT", 3, 1, 1)
            router(1)
            rows(3, "gate", 5, (LATENT,))
            ranks(1)
            experts(1)

        @block.scalar
        def _(act):
            step = chained(act, act_step)

            def drain(out, bank, func=ACT.Copy, **kw):
                act.activation(out, bank, func, **kw).then_inc(act_drained, 1)

            for s, name in ((LATENT, "c"), (CONTEXT, "c_ctx")):
                src = A[name][0] if name == "c" else A[name]
                for a in (0, 1):
                    act.dma_start(craw[:, s, 4 * a:4 * a + 4],
                                  src[512 * a:512 * (a + 1)].rearrange("(p j) -> p j", j=4)).then_inc(ld_c, 16)
            at_row = 0
            for name, n in (("even_dw", TAPS), ("even_dw_b", 1), ("even_ln_g", 1), ("even_ln_b", 1), ("odd_conv", 3)):
                src = A[name][0] if n > 1 else A[name]
                act.dma_start(chan_rows[at_row:at_row + n, :], src).then_inc(ld_rows, 16)
                at_row += n

            def layer_rows(l):
                for s in (LATENT, CONTEXT):
                    act.dma_start(modrow[s:P:32, :, :],
                                  A["b_mod"][l].rearrange("(v j n) -> j v n", j=4, n=BLK)).then_inc(ld_bmod, 16)
                    for k, name in enumerate(("norm_mix", "norm_ffn")):
                        act.dma_start(grow[s:P:32, k, :],
                                      A[name][l].rearrange("(j n) -> j n", n=BLK)).then_inc(ld_bmod, 16)

            def router_weights(l):
                for a in (0, 1):
                    half = slice(512 * a, 512 * (a + 1))
                    act.dma_start(WR[:, 4 * a:4 * a + 4, 0:GROUPS],
                                  A["moe_wg"][l, half, :].rearrange("(p j) n -> p j n", j=4)).then_inc(ld_router, 16)
                    act.dma_start(WR[:, 4 * a:4 * a + 4, GROUPS:],
                                  A["moe_we"][l, half, :].rearrange("(p j) n -> p j n", j=4)).then_inc(ld_router, 16)
                act.dma_start(RB[:, 0:GROUPS], A["moe_bg"][l:l + 1, :].broadcast_to([P, GROUPS])).then_inc(ld_router, 16)
                act.dma_start(RB[:, GROUPS:], A["moe_be"][l:l + 1, :].broadcast_to([P, EXPERTS])).then_inc(ld_router, 16)

            def position_bias(h):
                rpb = A["even_rpb"]
                rows, cols = rpb.shape[2:]
                for half, row in ((0, 5), (1, 4)):
                    src = bass.AP(rpb.tensor, (h * rows + row) * cols + WIN_COLS - GRID_W,
                                  [[1, GRID_W], [cols, 6], [1, GRID_W]])
                    act.dma_start(BIAS[64 * half:64 * half + 64, h % 4, :, :], src).then_inc(ld_bias[h % 4], 16)

            act.wait_ge(zeroed, 1)
            layer_rows(0)
            act.wait_ge(ld_c, 64)
            act.wait_ge(dve_zeroed, 1)
            act.activation(csilu[:, :, 0:2], craw[:, :, :].rearrange("p s c -> p c s"), ACT.Silu).then_inc(c_silu, 1)
            for h in range(4):
                position_bias(h)
            router_weights(0)
            act.dma_start(subln, A["odd_subln"].rearrange("o p -> p o")).then_inc(ld_lam, 16)

            def norm(k):
                for t in range(norm_tiles[k]):
                    if k == 0:
                        act.wait_ge(ld_x, 32)
                    elif k in (2, 4):
                        act.wait_ge(x_updated, xu_moe[k // 2 - 1] - (norm_tiles[k] - 1 - t) if k == 4
                                    else xu_moe[0] - (3 - t))
                    else:
                        act.wait_ge(x_updated, xu_mix[k // 2])
                    step(act.activation(H[:, t, :], X[:, t, :], ACT.Square, accum_out=sumsq[:, k, t:t + 1]), wait=False)
                step.sync()
                act.activation(root[:, k, 0:norm_tiles[k]], sumsq[:, k, 0:norm_tiles[k]], ACT.Sqrt,
                               scale=1.0 / D, bias=eps).then_inc(norm_root, 1)

            def shift_rows(k, streams=(LATENT, CONTEXT)):
                for s in streams:
                    for hf in (0, 1):
                        drain(SHIFT[:, s, 512 * hf:512 * (hf + 1)], full(act, "row", k, "shift", s, hf))

            def gate_rows(k, streams=(LATENT, CONTEXT)):
                for s in streams:
                    for hf in (0, 1):
                        drain(G[:, s, 512 * hf:512 * (hf + 1)], full(act, "row", k, "gate", s, hf))

            def transposed(k, store=None):
                for t in range(norm_tiles[k]):
                    if store is not None:
                        act.wait_ge(h_ready, h_before[k] + t + 1)
                        act.dma_start(hrow[store][2 * P * t:2 * P * (t + 1), :].rearrange("(p r) d -> p (r d)", r=2),
                                      H[:, t, :]).then_inc(h_stored, 16)
                    bank = full(act, "hT", k, t, 1)
                    drain(hT[:, 4:8, P * t:P * (t + 1)], bank.rearrange("p (j t) -> p j t", j=4))

            def router_exps(l):
                act.wait_ge(router_max, l + 1)
                act.activation(rexp[:, :, :], rarg[:, :, :], ACT.Exp).then_inc(router_exp, 1)

            extras = act.alloc_register("act_extras")
            act.reg_mov(extras, 0)

            def experts(l):
                n0 = EXPERTS * l

                def copy_xT(i, q):
                    n, b = i * PER_LOOP + (n0 + q), q % 2
                    act.wait_ge(xT_full, n + 1)
                    act.activation(XT[:, b, :, :, :].rearrange("p j a s -> p (j a s)"), ps[:, b, :],
                                   ACT.Copy).then_inc(xT_ready, 1)

                def silu(i, q):
                    n, b = i * PER_LOOP + (n0 + q), q % 2
                    act.wait_ge(up_full, n + 1)
                    act.activation(SA[:, b, :], ps[0:CAP, 2 + b, 0:BLK], ACT.Silu).then_inc(gate_ready, 1)

                def copy_y(i, q):
                    n, b = i * PER_LOOP + (n0 + q), q % 2
                    act.wait_ge(y_full, n + 1)
                    act.wait_ge(scattered[b], (i * 2 + (n0 + q) // 2) * 16)
                    act.activation(YS[:, b, :], ps[:, 5 + b, :], ACT.Copy).then_inc(y_ready, 1)

                def more(q, count):
                    bank = ps[:, 7, :]
                    with act.If(count > 0):
                        with act.Fori(0, count):
                            act.reg_add(extras, extras, 1)
                            x = act.snap(extras)
                            act.wait_ge(x_xT_full, x)
                            act.activation(XTX.rearrange("p j a s -> p (j a s)"), bank, ACT.Copy).then_inc(x_xT_ready, 1)
                            act.wait_ge(x_up_full, x)
                            act.activation(SAX, bank[0:CAP, 0:BLK], ACT.Silu).then_inc(x_gate_ready, 1)
                            act.wait_ge(x_y_full, x)
                            act.activation(YSX, bank, ACT.Copy).then_inc(x_y_ready, 1)

                def one(i, q, count, ahead2=True, ahead1=True):
                    if ahead2:
                        copy_xT(*job_after(i, q, 2))
                    if ahead1:
                        silu(*job_after(i, q, 1))
                    copy_y(i, q)
                    more(q, count)

                copy_xT(0, 0)
                copy_xT(0, 1)
                silu(0, 0)
                act.wait_ge(extra_ready, l + 1)
                last = EXPERTS // PER_LOOP - 1
                with act.Fori(0, last) as i:
                    c = extra_counts(act, l, i)
                    for q in range(PER_LOOP):
                        one(i, q, c[q])
                c = extra_counts(act, l, last)
                for q in range(PER_LOOP):
                    one(last, q, c[q], ahead2=(q < 2), ahead1=(q < 3))

            norm(0)
            shift_rows(0)
            transposed(0)
            act.wait_ge(z_clear, 1)
            for what, b, _ in EVEN_BLOCKS:
                for f in (0, 1):
                    if what == "u":
                        bank = full(act, what, b, f)
                        drain(Z[:, 2 * b + f, :, PAD:PAD + SEQ], bank.rearrange("p (s t) -> p s t", s=2))
                    elif what == "g":
                        ct = 2 * b + f
                        bank = full(act, what, b, f)
                        if ct >= 2:
                            act.wait_ge(gated_in, ct - 1)
                        drain(SG[:, ct % 2, :], bank, ACT.Sigmoid)
                    elif what == "q":
                        drain(QK[:, 2 * b + f, :], full(act, what, b, f), scale=A_DIM ** -0.5)
                    elif what == "k":
                        drain(QK[:, 4 + 2 * b + f, :], full(act, what, b, f))
                    else:
                        bank = full(act, what, b, f)
                        drain(V[:, 2 * f:2 * f + 2, BLK * b:BLK * (b + 1)], bank.rearrange("p (t n) -> p t n", t=2))

            def exps(n):
                act.wait_ge(max_ready, n + 1)
                bank = ps[:, plan["S", n]["bank"], :]
                keys = slice(0 if n % 4 < 2 else SEQ, TOK)
                drain(PR[:, n % 2, keys], bank[:, keys], ACT.Exp, bias=nmax[:, n:n + 1],
                      accum_out=sums[:, n % 4:n % 4 + 1])
                if n % 4 == 1 and n // 4 + 4 < A_HEADS:
                    position_bias(n // 4 + 4)

            units = 4 * A_HEADS
            act.wait_ge(gated_in, 4)
            exps(0)
            exps(1)
            for n in range(units):
                h, qt = n // 4, n % 4
                bank = full(act, "PT", n)
                if qt == 0 and h >= 1:
                    full(act, "O", h - 1)
                if qt < 2:
                    drain(PTX[:, :, P * qt:P * (qt + 1)], bank.rearrange("p (k q) -> p k q", k=4))
                else:
                    drain(PTC[:, :, P * (qt - 2):P * (qt - 1)], bank[:, SEQ:TOK].rearrange("p (k q) -> p k q", k=2))
                if n + 2 < units:
                    exps(n + 2)
                if qt == 3:
                    p0 = A_DIM * (h % 2)
                    drain(aT[p0:p0 + A_DIM, h // 2, :], full(act, "O", h)[p0:p0 + A_DIM, :])
            for ct in range(4):
                act.wait_ge(centred, ct + 1)
                act.activation(SQ[:, ct, :], Y[:, ct, :], ACT.Square).then_inc(squared, 1)
            drain(SD, full(act, "var"), ACT.Sqrt, scale=1.0 / 512, bias=eps)
            for ct in range(4):
                act.wait_ge(ln_scaled, ct + 1)
                act.activation(Y[:, ct, :], Y[:, ct, :], ACT.Silu, scale=chan[:, ct, 32:33],
                               bias=chan[:, ct, 33:34]).then_inc(b_ready, 1)
            gate_rows(0)
            shift_rows(1)
            norm(1)
            transposed(1, store=0)
            router_exps(0)
            drained(act, "out", 0, 3, 1)
            gate_rows(1)
            layer_rows(1)
            drained(act, "logit", 0)
            router_weights(1)
            act.dma_start(BIASF[:, 0:512], A["rotary"]).then_inc(ld_rot, 16)
            act.dma_start(LAMROW, A["odd_lambda"].rearrange("o a b -> o (a b)").broadcast_to([P, 256])).then_inc(ld_lam, 16)
            experts(0)


            act.wait_ge(x_updated, xu_moe[0])
            shift_rows(2)
            norm(2)
            act.wait_ge(lam_sums, 1)
            act.activation(lam[:, 2:4], lam[:, 0:2], ACT.Exp).then_inc(lam_exp, 1)
            transposed(2)
            for what, b, _ in ODD_BLOCKS:
                if what in ("cu", "cb"):
                    continue
                if what == "cc":
                    drain(CC[:, 2 * b:2 * b + 2, :], full(act, what, b).rearrange("p (c t) -> p c t", c=2))
                    continue
                for f in (0, 1):
                    bank = full(act, what, b, f)
                    if what == "dq":
                        drain(DQ[:, 2 * b + f, :], bank[:, 0:SEQ], scale=64 ** -0.5)
                    elif what == "dk":
                        drain(DK[:, 2 * b + f, :], bank)
                    else:
                        drain(V[:, 2 * f:2 * f + 2, BLK * b:BLK * (b + 1)], bank.rearrange("p (t n) -> p t n", t=2))

            def diff_exps(n):
                act.wait_ge(max_ready, units + n + 1)
                for m in (0, 1):
                    drain(DP[:, 2 * (n % 2) + m, :], ps[:, plan["DS", n, m]["bank"], :], ACT.Exp,
                          bias=nmax[:, 2 * n + m:2 * n + m + 1], accum_out=sums[:, 2 * (n % 4) + m:2 * (n % 4) + m + 1])

            diff_exps(0)
            for n in range(2 * D_HEADS):
                if n + 1 < 2 * D_HEADS:
                    diff_exps(n + 1)
                bank = full(act, "DPT", n)
                if n >= 2:
                    full(act, "DO", n - 2)
                drain(DPT[:, n % 2, :, :], bank.rearrange("p (k q) -> p k q", k=4))
            act.wait_ge(o_squared, 2 * D_HEADS)
            act.activation(droot, dss, ACT.Sqrt, scale=1.0 / P, bias=eps).then_inc(o_root, 1)
            for n in range(2 * D_HEADS):
                h, qt = n // 2, n % 2
                drain(dT[:, h, P * qt:P * (qt + 1)], full(act, "DT", n)[:, 0:P], ACT.Identity, scale=sublns)
            gate_rows(2, (LATENT,))
            shift_rows(3, (LATENT,))
            norm(3)
            transposed(3, store=1)
            router_exps(1)
            drained(act, "out", 1, 3, 0)
            gate_rows(3, (LATENT,))
            act.dma_start(GF, A["norm_final"].rearrange("(o d) -> o d", o=1).broadcast_to([P, D])).then_inc(ld_final, 16)
            experts(1)
            norm(4)
            for t in (0, 1):
                act.wait_ge(final_ready, t + 1)
                act.dma_start(A["out"][0, P * t:P * (t + 1), :], H[:, t, :]).then_inc(stored, 16)

        @block.vector
        def _(dve):
            step = chained(dve, dve_step)

            def done(ins):
                ins.then_inc(dve_drained, 1)

            step(dve.memset(eps, EPS))
            dve.memset(csilu[:, :, :], 0.0).then_inc(dve_zeroed, 1)
            bank = full(dve, "chan")[:, 0:160].rearrange("p (c k) -> p c k", c=4)
            done(dve.tensor_copy(chan[:, :, 0:37], bank[:, :, 0:37]))

            def modulation(l, v):
                bank = full(dve, "mod", l, v)
                dve.wait_ge(ld_bmod, 96 * (l + 1))
                done(dve.tensor_tensor(modrow[:, v, :], bank[:, 0:BLK], modrow[:, v, :], ALU.add))
                if v in (1, 4):
                    drained(dve, "mod", l, v)
                    dve.scalar_tensor_tensor(out=modrow[:, v, :], in0=modrow[:, v, :], scalar=1.0,
                                             in1=grow[:, v // 4, :], op0=ALU.add, op1=ALU.mult).then_inc(row_scale, 1)

            def scale_rows(k, streams=(LATENT, CONTEXT)):
                for s in streams:
                    for hf in (0, 1):
                        done(dve.tensor_copy(SCALE[:, s, 512 * hf:512 * (hf + 1)], full(dve, "row", k, "scale", s, hf)))

            def norm(k):
                T = norm_tiles[k]
                dve.wait_ge(norm_root, k + 1)
                step(dve.reciprocal(rstd[:, k, 0:T], root[:, k, 0:T]))
                if k < 4:
                    drained(dve, "row", k, "scale", CONTEXT if k < 3 else LATENT, 1)
                else:
                    dve.wait_ge(ld_final, 16)
                for t in range(T):
                    g = SCALE[:, t // 2, :] if k < 4 else GF
                    dve.scalar_tensor_tensor(out=H[:, t, :], in0=X[:, t, :], scalar=rstd[:, k, t:t + 1], in1=g,
                                             op0=ALU.mult, op1=ALU.mult).then_inc(h_scaled if k < 4 else final_ready, 1)

            def transposed(k):
                for t in range(norm_tiles[k]):
                    bank = full(dve, "hT", k, t, 0)
                    done(dve.tensor_copy(hT[:, 0:4, P * t:P * (t + 1)], bank.rearrange("p (j t) -> p j t", j=4)))

            def gated_output(l):
                for b in range(4):
                    for tp in range(tiles_of[l] // 2):
                        i = b * (tiles_of[l] // 2) + tp
                        bank = full(dve, "out", l, b, tp)
                        drained(dve, "row", 2 * l, "gate", CONTEXT if l == 0 else LATENT, 1)
                        if i >= 2:
                            dve.wait_ge(x_updated, (0, xu_moe[0])[l] + i - 1)
                        g = G[:, tp, BLK * b:BLK * (b + 1)].unsqueeze(1).broadcast_to([P, 2, BLK])
                        done(dve.tensor_tensor(PR[:, i % 2, :].rearrange("p (t n) -> p t n", t=2),
                                               bank.rearrange("p (t n) -> p t n", t=2), g, ALU.mult))

            def first_of(value, best, hot, T):
                c = cand[:, 0:T, :]
                step(dve.tensor_tensor(c, value[:, 0:T, :], best[:, 0:T].unsqueeze(2).broadcast_to([P, T, EXPERTS]), ALU.is_equal))
                step(dve.scalar_tensor_tensor(out=c, in0=c, scalar=-100.0, in1=iota.unsqueeze(1).broadcast_to([P, T, EXPERTS]),
                                              op0=ALU.mult, op1=ALU.add))
                step(dve.tensor_reduce(least[:, 0:T], c, AX.X, ALU.min))
                step(dve.tensor_tensor(hot[:, 0:T, :], c, least[:, 0:T].unsqueeze(2).broadcast_to([P, T, EXPERTS]), ALU.is_equal))

            def route(l):
                T = tiles_of[l]
                lg = logits[:, 0:T, :]
                bank = full(dve, "logit", l)
                dve.wait_ge(ld_router, 96 * (l + 1))
                done(dve.tensor_tensor(lg, bank[:, 0:36 * T].rearrange("p (t n) -> p t n", t=T),
                                       RB[:, :].unsqueeze(1).broadcast_to([P, T, GROUPS + EXPERTS]), ALU.add))
                drained(dve, "logit", l)
                g = lg[:, :, 0:GROUPS]
                step(dve.tensor_reduce(gmax[:, 0:T], g, AX.X, ALU.max))
                if T < 4:
                    step(dve.memset(rarg[:, :, :], 0.0))
                step(dve.tensor_tensor(rarg[:, 0:T, :], g, gmax[:, 0:T].unsqueeze(2).broadcast_to([P, T, GROUPS]), ALU.subtract))
                gc, gh, gp = gcand[:, 0:T, :], ghot[:, 0:T, :], gpen[:, 0:T, :]
                step(dve.tensor_scalar(gc, rarg[:, 0:T, :], 0.0, None, ALU.is_ge))
                step(dve.scalar_tensor_tensor(out=gc, in0=gc, scalar=-100.0,
                                              in1=iota[:, 0:GROUPS].unsqueeze(1).broadcast_to([P, T, GROUPS]),
                                              op0=ALU.mult, op1=ALU.add))
                step(dve.tensor_reduce(least[:, 0:T], gc, AX.X, ALU.min))
                step(dve.tensor_tensor(gh, gc, least[:, 0:T].unsqueeze(2).broadcast_to([P, T, GROUPS]), ALU.is_equal))
                step(dve.tensor_scalar(gp, gh, -NEG, NEG, ALU.mult, ALU.add))
                for t in range(T):
                    m = masked[:, t, :].rearrange("p (g e) -> p g e", g=GROUPS)
                    step(dve.tensor_tensor(m, lg[:, t, GROUPS:].rearrange("p (g e) -> p g e", g=GROUPS),
                                           gh[:, t, :].unsqueeze(2).broadcast_to([P, GROUPS, PER_GROUP]), ALU.mult), wait=False)
                step.sync()
                for t in range(T):
                    m = masked[:, t, :].rearrange("p (g e) -> p g e", g=GROUPS)
                    step(dve.tensor_tensor(m, m, gp[:, t, :].unsqueeze(2).broadcast_to([P, GROUPS, PER_GROUP]), ALU.add), wait=False)
                step.sync()
                step(dve.tensor_reduce(emax[:, 0:T], masked[:, 0:T, :], AX.X, ALU.max))
                first_of(masked, emax, first_choice, T)
                step(dve.scalar_tensor_tensor(out=masked[:, 0:T, :], in0=first_choice[:, 0:T, :], scalar=NEG,
                                              in1=masked[:, 0:T, :], op0=ALU.mult, op1=ALU.add))
                step(dve.tensor_reduce(emax2[:, 0:T], masked[:, 0:T, :], AX.X, ALU.max))
                first_of(masked, emax2, second_choice, T)
                dve.tensor_tensor(chosen[:, 0:T, :], first_choice[:, 0:T, :], second_choice[:, 0:T, :],
                                  ALU.add).then_inc(one_hot, 1)
                dve.tensor_tensor(rarg[:, 4, 0:T], emax2[:, 0:T], emax[:, 0:T], ALU.subtract).then_inc(router_max, 1)
                dve.wait_ge(router_exp, l + 1)
                step(dve.tensor_reduce(gsum[:, 0:T], rexp[:, 0:T, :], AX.X, ALU.add))
                step(dve.scalar_tensor_tensor(out=gsum[:, 0:T], in0=rexp[:, 4, 0:T], scalar=1.0, in1=gsum[:, 0:T],
                                              op0=ALU.add, op1=ALU.mult))
                step(dve.reciprocal(topw[:, 0:T, 0], gsum[:, 0:T]))
                step(dve.tensor_tensor(topw[:, 0:T, 1], rexp[:, 4, 0:T], topw[:, 0:T, 0], ALU.mult))
                bank = full(dve, "rank", l)
                step(dve.scalar_tensor_tensor(out=place[:, 0:T, :], in0=bank[:, 0:EXPERTS * T].rearrange("p (t e) -> p t e", t=T),
                                              scalar=float(EXPERTS), in1=iota.unsqueeze(1).broadcast_to([P, T, EXPERTS]),
                                              op0=ALU.mult, op1=ALU.add))
                done(dve.tensor_copy(count[0:1, :], bank[0:1, EXPERTS * 4:EXPERTS * 5]))
                for k, hot in enumerate((first_choice, second_choice)):
                    step(dve.tensor_tensor(cand[:, 0:T, :], hot[:, 0:T, :], place[:, 0:T, :], ALU.mult))
                    step(dve.tensor_reduce(pos_f[:, 0:T], cand[:, 0:T, :], AX.X, ALU.add))
                    ins = dve.tensor_copy(pos_i[:, l, 0:T, k], pos_f[:, 0:T])
                    if k == 0:
                        step(ins)
                    else:
                        ins.then_inc(pos_ready, 1)
                drained(dve, "rank", l)
                step(dve.tensor_scalar(blocks[0:1, :], count[0:1, :], float(CAP), None, ALU.is_gt))
                for b in range(2, T * P // CAP):
                    step(dve.scalar_tensor_tensor(out=blocks[0:1, :], in0=count[0:1, :], scalar=float(CAP * b),
                                                  in1=blocks[0:1, :], op0=ALU.is_gt, op1=ALU.add))
                step(dve.tensor_tensor(packed[0:1, :], blocks[0:1, :], const[0:1, C_POW:C_POW + EXPERTS], ALU.mult))
                step(dve.tensor_reduce(words[0:1, :], packed[0:1, :].rearrange("p (w e) -> p w e", e=PER_LOOP), AX.X, ALU.add))
                dve.tensor_copy(extra_i[0:1, l, :], words[0:1, :]).then_inc(extra_ready, 1)

            extras = dve.alloc_register("dve_extras")
            dve.reg_mov(extras, 0)

            def experts(l):
                n0 = EXPERTS * l

                def hidden(i, q):
                    n, b = i * PER_LOOP + (n0 + q), q % 2
                    dve.wait_ge(gate_ready, n + 1)
                    dve.tensor_tensor(HID[:, b, :], SA[:, b, :], ps[CAP:P, 2 + b, 0:BLK], ALU.mult).then_inc(hid_ready, 1)

                def copy_hT(i, q):
                    n, b = i * PER_LOOP + (n0 + q), q % 2
                    dve.wait_ge(hidT_full, n + 1)
                    dve.tensor_copy(HT[:, b, :, :].rearrange("p f s -> p (f s)"),
                                    ps[:, 4, P * b:P * (b + 1)]).then_inc(hidT_ready, 1)

                def more(q, count):
                    bank = ps[:, 7, :]
                    with dve.If(count > 0):
                        with dve.Fori(0, count):
                            dve.reg_add(extras, extras, 1)
                            x = dve.snap(extras)
                            dve.wait_ge(x_gate_ready, x)
                            dve.tensor_tensor(HIDX, SAX, bank[CAP:P, 0:BLK], ALU.mult).then_inc(x_hid_ready, 1)
                            dve.wait_ge(x_hidT_full, x)
                            dve.tensor_copy(HTX.rearrange("p f s -> p (f s)"), bank[:, 0:P]).then_inc(x_hidT_ready, 1)

                def one(i, q, count, ahead=True):
                    copy_hT(i, q)
                    if ahead:
                        hidden(*job_after(i, q, 1))
                    more(q, count)

                hidden(0, 0)
                dve.wait_ge(extra_ready, l + 1)
                last = EXPERTS // PER_LOOP - 1
                with dve.Fori(0, last) as i:
                    c = extra_counts(dve, l, i)
                    for q in range(PER_LOOP):
                        one(i, q, c[q])
                c = extra_counts(dve, l, last)
                for q in range(PER_LOOP):
                    one(last, q, c[q], ahead=(q < 3))

            def combine(l):
                for t in range(tiles_of[l]):
                    dve.wait_ge(y_back[t % 2], 16 * ((t // 2 + 1) + (2 if l else 0)))
                    g = G[:, t // 2, :]
                    for k in (0, 1):
                        step(dve.scalar_tensor_tensor(out=YP[:, t % 2, k, :], in0=YP[:, t % 2, k, :],
                                                      scalar=topw[:, t, k:k + 1], in1=g, op0=ALU.mult, op1=ALU.mult), wait=False)
                    step.sync()
                    dve.tensor_tensor(YP[:, t % 2, 0, :], YP[:, t % 2, 0, :], YP[:, t % 2, 1, :],
                                      ALU.add).then_inc(combined, 1)

            modulation(0, 0)
            modulation(0, 1)
            scale_rows(0)
            norm(0)
            transposed(0)

            def taps(ct, k):
                out = Y[:, ct, :].rearrange("p (s t) -> p s t", s=2)
                z = Z[:, ct, :, k:k + SEQ]
                if k == 0:
                    return dve.tensor_scalar(out, z, chan[:, ct, 0:1], chan[:, ct, TAPS:TAPS + 1], ALU.mult, ALU.add)
                return dve.scalar_tensor_tensor(out=out, in0=z, scalar=chan[:, ct, k:k + 1], in1=out,
                                                op0=ALU.mult, op1=ALU.add)


            def maxima(n):
                bank = full(dve, "S", n)
                if n >= 1:
                    dve.wait_ge(max_ready, n)
                step(dve.tensor_reduce(m1, bank[:, 0 if n % 4 < 2 else SEQ:TOK], AX.X, ALU.max))
                dve.tensor_scalar(nmax[:, n:n + 1], m1, -1.0, None, ALU.mult).then_inc(max_ready, 1)

            def diagonal(n):
                drained(dve, "S", n)
                r = rsum[:, 0:1]
                if n >= 1:
                    dve.wait_ge(diag_ready, n)
                if n >= 2:
                    full(dve, "PT", n - 2)
                step(dve.reciprocal(r, sums[:, n % 4:n % 4 + 1]))
                dve.tensor_scalar(diag[:, n % 2, :], ident, r, None, ALU.mult).then_inc(diag_ready, 1)

            units = 4 * A_HEADS
            maxima(0)
            maxima(1)
            for n in range(units):
                diagonal(n)
                if n + 2 < units:
                    maxima(n + 2)
                if n < TAPS:
                    if n == 0:
                        dve.wait_ge(gated_in, 4)
                    for ct in range(4):
                        if n:
                            dve.wait_ge(conv_step, 4 * (n - 1) + ct + 1)
                        taps(ct, n).then_inc(conv_step, 1)
                if n % 4 == 3 and 2 + n // 4 < MOD_PER_LAYER:
                    modulation(0, 2 + n // 4)
            bank = full(dve, "mean")
            for ct in range(4):
                ins = dve.scalar_tensor_tensor(out=Y[:, ct, :], in0=bank, scalar=-1.0 / 512, in1=Y[:, ct, :],
                                               op0=ALU.mult, op1=ALU.add)
                ins.then_inc(centred, 1)
            done(dve.tensor_copy(m1, bank[:, 0:1]))
            drained(dve, "var")
            step(dve.reciprocal(SD, SD))
            for ct in range(4):
                dve.tensor_tensor(Y[:, ct, :], Y[:, ct, :], SD, ALU.mult).then_inc(ln_scaled, 1)
            dve.wait_ge(ln_scaled, 4)
            gated_output(0)
            scale_rows(1)
            norm(1)
            transposed(1)
            route(0)
            for v in range(MOD_PER_LAYER):
                modulation(1, v)
            experts(0)
            combine(0)

            dve.wait_ge(x_updated, xu_moe[0])
            scale_rows(2)
            norm(2)
            dve.wait_ge(ld_lam, 32)
            for i in (0, 1):
                step(dve.tensor_tensor_reduce(PR[:, 1, 64 * i:64 * i + 64], LAMROW[:, 128 * i:128 * i + 64],
                                              LAMROW[:, 128 * i + 64:128 * i + 128], 1.0, 0.0, ALU.mult, ALU.add,
                                              lam[:, i:i + 1]), wait=False)
            dve.tensor_scalar(sublns, subln, 1.0 - LAM_INIT, None, ALU.mult).then_inc(lam_sums, 1)
            transposed(2)
            dve.wait_ge(lam_exp, 1)
            step(dve.tensor_tensor(lam[:, 4:5], lam[:, 3:4], lam[:, 2:3], ALU.subtract))
            step(dve.tensor_scalar(lam[:, 5:6], lam[:, 4:5], -LAM_INIT, None, ALU.add))
            for col in (0, SEQ + 1):
                step(dve.memset(CU[:, :, col:col + 1], 0.0))
            dve.wait_ge(ld_rot, 16)
            tile = 0
            for what, b, _ in ODD_BLOCKS:
                if what in ("dq", "dk"):
                    for f in (0, 1):
                        x = (DQ if what == "dq" else DK)[:, 2 * b + f, 0:SEQ]
                        r = ROT[:, tile % 2, 0:SEQ]
                        bank = full(dve, what + "swap", b, f)
                        if tile >= 2:
                            dve.wait_ge(rot_ready, tile - 1)
                        done(dve.tensor_tensor(r, bank[:, 0:SEQ], SIN, ALU.mult))
                        step(dve.tensor_tensor(x, x, COS, ALU.mult))
                        drained(dve, what + "swap", b, f)
                        dve.tensor_tensor(x, x, r, ALU.add).then_inc(rot_ready, 1)
                        tile += 1
                elif what == "cu":
                    drained(dve, "cc", b)
                    done(dve.tensor_tensor(CU[:, 2 * b:2 * b + 2, 1:1 + SEQ],
                                           full(dve, "cu", b).rearrange("p (c t) -> p c t", c=2),
                                           CC[:, 2 * b:2 * b + 2, :], ALU.mult))
                    drained(dve, "cu", b)
                    for k in range(3):
                        for ct in (2 * b, 2 * b + 1):
                            z, w = CU[:, ct, k:k + SEQ], chan[:, ct, 34 + k:35 + k]
                            if k == 0:
                                step(dve.tensor_scalar(CV[:, ct, :], z, w, None, ALU.mult), wait=False)
                            else:
                                step(dve.scalar_tensor_tensor(out=CV[:, ct, :], in0=z, scalar=w, in1=CV[:, ct, :],
                                                              op0=ALU.mult, op1=ALU.add), wait=False)
                        step.sync()
                elif what == "cb":
                    cv = CV[:, 2 * b:2 * b + 2, :]
                    done(dve.tensor_tensor(cv, full(dve, "cb", b).rearrange("p (c t) -> p c t", c=2), cv, ALU.mult))

            def diff_maxima(n):
                banks = [full(dve, "DS", n, m) for m in (0, 1)]
                for m in (0, 1):
                    step(dve.tensor_reduce((m1, m2)[m], banks[m], AX.X, ALU.max), wait=False)
                step.sync()
                dve.tensor_scalar(nmax[:, 2 * n:2 * n + 2], small[:, 96:98], -1.0, None, ALU.mult).then_inc(max_ready, 1)
                dve.wait_ge(max_ready, units + n + 1)

            def diff_diagonals(n):
                drained(dve, "DS", n, 1)
                if n >= 2:
                    full(dve, "DPT", n - 2)
                if n >= 1:
                    dve.wait_ge(diag_ready, units + n)
                k = 2 * (n % 4)
                step(dve.reciprocal(rsum[:, 0:2], sums[:, k:k + 2]))
                step(dve.tensor_tensor(rsum[:, 2:3], rsum[:, 1:2], lam[:, 5:6], ALU.mult))
                step(dve.tensor_scalar(diag[:, 2 * (n % 2), :], ident, rsum[:, 0:1], None, ALU.mult), wait=False)
                dve.tensor_scalar(diag[:, 2 * (n % 2) + 1, :], ident, rsum[:, 2:3], None, ALU.mult).then_inc(diag_ready, 1)

            diff_maxima(0)
            for n in range(2 * D_HEADS):
                diff_diagonals(n)
                if n + 1 < 2 * D_HEADS:
                    diff_maxima(n + 1)
                done(dve.tensor_copy(OD[:, n, :], full(dve, "DO", n)[:, 0:P]))
                drained(dve, "DO", n)
                scratch = RM[:, P * n:P * (n + 1)]
                dve.tensor_tensor_reduce(scratch, OD[:, n, :], OD[:, n, :], 1.0, 0.0, ALU.mult, ALU.add,
                                         dss[:, n:n + 1]).then_inc(o_squared, 1)
            dve.wait_ge(o_root, 1)
            step(dve.reciprocal(drstd, droot))
            for n in range(2 * D_HEADS):
                if n >= 4:
                    full(dve, "DT", n - 4)
                dve.tensor_scalar(diag[:, n % 4, :], ident, drstd[:, n:n + 1], None, ALU.mult).then_inc(odiag, 1)
            gated_output(1)
            scale_rows(3, (LATENT,))
            norm(3)
            transposed(3)
            route(1)
            experts(1)
            combine(1)
            norm(4)

        @block.gpsimd
        def _(pool):
            step = chained(pool, pool_step)
            step(pool.memset(modrow[:, :, :], 0.0), wait=False)
            pool.memset(grow[:, :, :], 0.0).then_inc(zeroed, 1)
            step(pool.memset(skip_i[:, :], SKIP))
            for l in (0, 1):
                pool.dma_start(table[l].rearrange("(p r) k -> p (r k)", p=P),
                               skip_i[:, 0:tokens[l] // 2]).then_inc(table_set, 16)
            pool.memset(RM[:, :], 0.0).then_inc(z_clear, 1)
            pool.wait_ge(ld_const, 16)
            step(pool.tensor_copy(val_i[:, :, :, :].rearrange("p t k v -> p (t k v)"), const[:, C_VAL:C_VAL + 16]))

            def norm(k):
                for t in range(norm_tiles[k]):
                    pool.wait_ge(h_scaled, h_before[k] + t + 1)
                    drained(pool, "row", k, "shift", t // 2, 1)
                    pool.tensor_tensor(H[:, t, :], H[:, t, :], SHIFT[:, t // 2, :], ALU.add).then_inc(h_ready, 1)

            def mask(h):
                pool.wait_ge(ld_bias[h % 4], 32 * (h // 4 + 1))
                for half in (0, 1):
                    b = BIAS[64 * half:64 * half + 64, h % 4, :, :]
                    lo, hi = b[:, :, 0:48], b[:, :, 16:64]
                    step(pool.affine_select(out=lo, in_=lo, compare_op=ALU.is_ge, fill=NEG, base=-55,
                                            pattern=[[0, 6], [1, 48]], channel_multiplier=1))
                    ins = pool.affine_select(out=hi, in_=hi, compare_op=ALU.is_ge, fill=NEG, base=54,
                                             pattern=[[0, 6], [-1, 48]], channel_multiplier=-1)
                    if half == 0:
                        step(ins)
                    else:
                        ins.then_inc(bias_ready, 1)
                pool.wait_ge(bias_ready, h + 1)

            def add_outputs(l):
                for b in range(4):
                    for tp in range(tiles_of[l] // 2):
                        i = b * (tiles_of[l] // 2) + tp
                        drained(pool, "out", l, b, tp)
                        x = X[:, 2 * tp:2 * tp + 2, BLK * b:BLK * (b + 1)]
                        pool.tensor_tensor(x, x, PR[:, i % 2, :].rearrange("p (t n) -> p t n", t=2),
                                           ALU.add).then_inc(x_updated, 1)

            def slot_table(l):
                T = tiles_of[l]
                pool.wait_ge(table_set, 32)
                pool.wait_ge(pos_ready, l + 1)
                for t in range(T):
                    for k in (0, 1):
                        pool.indirect_dma_start(
                            out=table[l], out_offset=bass.IndirectOffsetOnAxis(ap=pos_i[:, l, t, k:k + 1], axis=0),
                            in_=val_i[:, t, k, :], in_offset=None, bounds_check=tokens[l] * EXPERTS - 1,
                            oob_is_err=False).then_inc(table_written, 16)
                pool.wait_ge(table_written, 16 * 2 * (4 if l == 0 else 6))
                blocks = T * P // CAP
                for half in (0, 1):
                    pool.dma_start(idx[CAP * half:CAP * (half + 1), 0:blocks, :, :],
                                   table[l][0:blocks * CAP * EXPERTS, :].rearrange("(b s e) k -> s b (e k)", s=CAP, e=EXPERTS)
                                   ).then_inc(idx_raw, 16)
                pool.wait_ge(idx_raw, 32 * (l + 1))
                second = idx[CAP:P, 0:blocks, :, :].rearrange("p b e k -> p (b e k)")
                step(pool.tensor_scalar(second, second, 1, None, ALU.add))

            extras = pool.alloc_register("pool_extras")
            pool.reg_mov(extras, 0)

            def experts(l):
                n0 = EXPERTS * l
                pool.wait_ge(h_stored, 16 * (4 if l == 0 else 6))
                full(pool, "hT", 1 + 2 * l, tiles_of[l] - 1, 1)
                step(pool.memset(XG.rearrange("p b d -> p (b d)"), 0.0), wait=False)
                step(pool.memset(XGX, 0.0))

                def gather(i, q):
                    n = i * PER_LOOP + (n0 + q)
                    if not (isinstance(i, int) and i == 0):
                        pool.wait_ge(xT_full, n - 3)
                    e = i * PER_LOOP + q
                    col = idx[:, 0, e:e + 1, 0] if isinstance(e, int) else idx[:, 0, bass.ds(e, 1), 0]
                    pool.tensor_copy(GIDX[q % 4], col).then_inc(gidx_ready, 1)
                    pool.wait_ge(gidx_ready, n + 1)
                    pool.sem_inc(pool_passed, 1)
                    pool.indirect_dma_start(out=XG[:, q % 4, :], out_offset=None, in_=hrow[l],
                                            in_offset=bass.IndirectOffsetOnAxis(ap=GIDX[q % 4], axis=0),
                                            bounds_check=2 * tokens[l] - 1, oob_is_err=False).then_inc(gathered[q % 4], 16)

                def scatter(i, q):
                    n, b = i * PER_LOOP + (n0 + q), q % 2
                    pool.wait_ge(y_ready, n + 1)
                    e = i * PER_LOOP + q
                    col = idx[:, 0, e:e + 1, 1] if isinstance(e, int) else idx[:, 0, bass.ds(e, 1), 1]
                    pool.tensor_copy(SIDX[b], col).then_inc(sidx_ready, 1)
                    pool.wait_ge(sidx_ready, n + 1)
                    pool.sem_inc(pool_passed, 1)
                    pool.indirect_dma_start(out=pair_out[l], out_offset=bass.IndirectOffsetOnAxis(ap=SIDX[b], axis=0),
                                            in_=YS[:, b, :], in_offset=None, bounds_check=4 * tokens[l] - 1,
                                            oob_is_err=False).then_inc(scattered[b], 16)

                def more(i, q, count):
                    e = i * PER_LOOP + q
                    with pool.If(count > 0):
                        with pool.Fori(0, count) as k:
                            pool.reg_add(extras, extras, 1)
                            x = pool.snap(extras)
                            for v, dst in ((0, GIDXX), (1, SIDXX)):
                                pool.tensor_copy(dst, idx[:, bass.ds(k + 1, 1), bass.ds(e, 1), v]
                                                 .rearrange("p b e -> p (b e)")).then_inc(x_gidx, 1)
                            pool.wait_ge(x_gidx, x * 2)
                            pool.sem_inc(pool_passed, 1)
                            pool.indirect_dma_start(out=XGX, out_offset=None, in_=hrow[l],
                                                    in_offset=bass.IndirectOffsetOnAxis(ap=GIDXX, axis=0),
                                                    bounds_check=2 * tokens[l] - 1, oob_is_err=False).then_inc(x_gathered, 16)
                            pool.wait_ge(x_y_ready, x)
                            pool.sem_inc(pool_passed, 1)
                            pool.indirect_dma_start(out=pair_out[l],
                                                    out_offset=bass.IndirectOffsetOnAxis(ap=SIDXX, axis=0),
                                                    in_=YSX, in_offset=None, bounds_check=4 * tokens[l] - 1,
                                                    oob_is_err=False).then_inc(x_scattered, 16)
                            pool.wait_ge(x_scattered, x * 16)

                def one(i, q, count, ahead=True):
                    if ahead:
                        gather(i + 1, q)
                    more(i, q, count)
                    scatter(i, q)

                for q in range(PER_LOOP):
                    gather(0, q)
                pool.wait_ge(extra_ready, l + 1)
                last = EXPERTS // PER_LOOP - 1
                with pool.Fori(0, last) as i:
                    c = extra_counts(pool, l, i)
                    for q in range(PER_LOOP):
                        one(i, q, c[q])
                c = extra_counts(pool, l, last)
                for q in range(PER_LOOP):
                    one(last, q, c[q], ahead=False)
                for b in (0, 1):
                    pool.wait_ge(scattered[b], 16 * (n0 + EXPERTS) // 2)

            def combine(l):
                T = tiles_of[l]

                def back(t):
                    pool.dma_start(YP[:, t % 2, :, :].rearrange("p k d -> p (k d)"),
                                   pair_out[l][4 * P * t:4 * P * (t + 1), :].rearrange("(p r) d -> p (r d)", r=4)
                                   ).then_inc(y_back[t % 2], 16)

                back(0)
                back(1)
                for t in range(T):
                    pool.wait_ge(combined, t + 1 + (4 if l else 0))
                    pool.tensor_tensor(X[:, t, :], X[:, t, :], YP[:, t % 2, 0, :], ALU.add).then_inc(x_updated, 1)
                    if t + 2 < T:
                        pool.wait_ge(x_updated, xu_moe[0] - T + t + 1)
                        back(t + 2)

            norm(0)
            for h in range(4):
                mask(h)
            for b in (0, 1):
                for f in (0, 1):
                    ct = 2 * b + f
                    drained(pool, "g", b, f)
                    z = Z[:, ct, :, PAD:PAD + SEQ]
                    pool.tensor_tensor(z, z, SG[:, ct % 2, :].rearrange("p (s t) -> p s t", s=2), ALU.mult).then_inc(gated_in, 1)
            for h in range(4, A_HEADS):
                mask(h)
            add_outputs(0)
            norm(1)
            slot_table(0)
            experts(0)
            combine(0)

            norm(2)
            add_outputs(1)
            norm(3)
            slot_table(1)
            experts(1)
            combine(1)


_INS = ["x", "c", "ctx", "c_ctx", "w_mod", "b_mod", "norm_mix", "norm_ffn", "norm_final",
        "even_w_in", "even_w_out", "even_rpb", "even_dw", "even_dw_b", "even_ln_g", "even_ln_b",
        "odd_w_in", "odd_w_out", "odd_conv", "odd_lambda", "odd_subln",
        "moe_wg", "moe_bg", "moe_we", "moe_be", "moe_w1", "moe_w3", "moe_w2"]


def kernel(**inputs):
    import concourse.bacc as _bacc
    from concourse.bass_utils import run_bass_kernel_spmd as _run

    nc = _bacc.Bacc("TRN2", target_bir_lowering=False, num_devices=1)
    consts, rotary = constants()
    arrays, aps = {}, {}
    for name, a in [(n, inputs[n]) for n in _INS] + [("consts", consts), ("rotary", rotary)]:
        a = np.ascontiguousarray(a)
        arrays[f"in_{name}"] = a
        aps[name] = nc.dram_tensor(f"in_{name}", a.shape, mybir.dt.from_np(a.dtype), kind="ExternalInput").ap()
    aps["out"] = nc.dram_tensor("out_x", (1, SEQ, D), F32, kind="ExternalOutput").ap()
    trunk(nc, aps)
    r = _run(nc, [arrays], core_ids=[0])
    return r.results[0]["out_x"]
```

```python
from contextlib import ExitStack

import numpy as np

import concourse.bass as bass
from concourse import mybir

F32 = mybir.dt.float32
I32 = mybir.dt.int32
F16 = mybir.dt.float16
ALU = mybir.AluOpType
ACT = mybir.ActivationFunctionType
AX = mybir.AxisListType

P = 128
D = 1024
SEQ = 256
CTX = 256
TOK = SEQ + CTX
NCH = D // P
GRID_W = 64
WIN_COLS = 16
EPS = 1e-6
NEG = -1e30
A_HEADS = 8
A_DIM = 64
TAPS = 31
PAD = TAPS // 2
D_HEADS = 4
LAM_INIT = 0.8 - 0.6 * float(np.exp(-0.3))
GROUPS = 4
PER_GROUP = 8
EXPERTS = GROUPS * PER_GROUP
BLK = 256
RING = 12
SLOT = NCH * BLK
PER_LOOP = 4
CAP = 64
NBLK = TOK // CAP
SKIP = 2048
MOD_PER_LAYER = 6
BANKS = 8

C_ID, C_SWAP, C_TRI, C_ONE, C_REV, C_IOTA, C_VAL, C_POW, C_OFF = 0, 128, 256, 384, 512, 640, 704, 720, 752
C_END = 756
LATENT, CONTEXT = 0, 1


def constants():
    c = np.zeros((P, C_END), np.float32)
    i = np.arange(P)
    c[i, C_ID + i] = 1.0
    c[i ^ 16, C_SWAP + i] = 1.0
    c[:, C_TRI:C_TRI + P] = i[:, None] < i[None, :]
    c[:, C_ONE:C_ONE + P] = 1.0
    c[i ^ 63, C_REV + i] = 1.0
    c[:, C_IOTA:C_IOTA + CAP] = np.arange(CAP)
    tok = np.arange(4)[None, :] * P + i[:, None]
    val = np.zeros((P, 2, 4, 2), np.float32)
    for k in (0, 1):
        val[:, k, :, 0] = 2 * tok - SKIP
        val[:, k, :, 1] = 2 * (2 * tok + k) - SKIP
    c[:, C_OFF] = SKIP + i // CAP
    c[:, C_VAL:C_VAL + 16] = val.reshape(P, 16)
    c[:, C_POW:C_POW + EXPERTS] = 8.0 ** (np.arange(EXPERTS) % PER_LOOP)
    quarter = 16
    inv = np.power(np.float32(10000.0), -np.arange(quarter, dtype=np.float32) / quarter).astype(np.float32)
    t = np.arange(SEQ)
    place = np.stack([t // GRID_W, t % GRID_W]).astype(np.float32)
    axis, half, f = (i % 64) // 32, (i % 32) // 16, i % 16
    ang = (place[axis] * inv[f][:, None]).astype(np.float32)
    rot = np.concatenate([np.cos(ang), np.sin(ang) * np.where(half == 0, -1.0, 1.0)[:, None]], 1)
    return c, rot.astype(np.float32)


TILE_ORDER = {4: (1, 0, 3, 2), 2: (1, 0)}
S_AHEAD = 3
MOD_AFTER = {5 * m + 4: lv for m, lv in enumerate([(0, 2), (0, 3), (0, 4), (0, 5), (1, 0), (1, 1)])}


def psum_plan():
    jobs = []

    def add(name, who):
        jobs.append((name, who))

    def row_vectors(k, what, who):
        for s in (LATENT, CONTEXT):
            for hf in (0, 1):
                add(("row", k, what, s, hf), who)

    def transposed(k, tiles):
        for t in TILE_ORDER[tiles]:
            for a in (0, 1):
                add(("hT", k, t, a), "act" if a else "dve")

    add(("chan",), "dve")
    add(("mod", 0, 1), "dve")
    row_vectors(0, "scale", "dve")
    add(("mod", 0, 0), "dve")
    row_vectors(0, "shift", "act")
    transposed(0, 4)
    for b in (0, 1):
        for what in ("u", "g"):
            for ft in (0, 1):
                add((what, b, ft), "act")
    for what in ("q", "k"):
        for b in (0, 1):
            for ft in (0, 1):
                add((what, b, ft), "act")
    for n in range(S_AHEAD):
        add(("S", n), "act")
    for b in (0, 1):
        for tp in (0, 1):
            add(("v", b, tp), "act")
    units = 4 * A_HEADS
    for n in range(units):
        add(("PT", n), "act")
        if n % 4 == 0 and n:
            add(("O", n // 4 - 1), "act")
        if n + S_AHEAD < units:
            add(("S", n + S_AHEAD), "act")
        if n in MOD_AFTER:
            add(("mod",) + MOD_AFTER[n], "dve")
    add(("O", A_HEADS - 1), "act")
    add(("mean",), "dve")
    row_vectors(0, "gate", "act")
    add(("mod", 1, 2), "dve")
    add(("var",), "act")
    for b in range(4):
        for tp in (0, 1):
            add(("out", 0, b, tp), "dve")
    row_vectors(1, "scale", "dve")
    row_vectors(1, "shift", "act")
    row_vectors(1, "gate", "act")
    add(("mod", 1, 3), "dve")
    add(("mod", 1, 4), "dve")
    transposed(1, 4)
    add(("logit", 0), "dve")
    add(("mod", 1, 5), "dve")
    add(("rank", 0), "dve")
    add(("slots", 0, 0), "dve")
    add(("slots", 0, 1), "dve")

    row_vectors(2, "scale", "dve")
    row_vectors(2, "shift", "act")
    transposed(2, 4)
    for what in ("dq", "dk"):
        for b in (0, 1):
            for ft in (0, 1):
                add((what, b, ft), "act")
                add((what + "swap", b, ft), "dve")
    for b in (0, 1):
        for tp in (0, 1):
            add(("dv", b, tp), "act")
    for n in (0, 1):
        for m in (0, 1):
            add(("DS", n, m), "act")
    for b in (0, 1):
        add(("cc", b), "act")
        add(("cu", b), "dve")
        add(("cb", b), "dve")
    for n in range(2 * D_HEADS):
        add(("DPT", n), "act")
        if n + 2 < 2 * D_HEADS:
            for m in (0, 1):
                add(("DS", n + 2, m), "act")
        if n >= 1:
            add(("DO", n - 1), "dve")
    add(("DO", 2 * D_HEADS - 1), "dve")
    for hf in (0, 1):
        add(("row", 2, "gate", LATENT, hf), "act")
    for n in range(2 * D_HEADS):
        add(("DT", n), "act")
    for b in range(4):
        add(("out", 1, b, 0), "dve")
    for what, who in (("scale", "dve"), ("shift", "act")):
        for hf in (0, 1):
            add(("row", 3, what, LATENT, hf), who)
    transposed(3, 2)
    add(("logit", 1), "dve")
    for hf in (0, 1):
        add(("row", 3, "gate", LATENT, hf), "act")
    add(("rank", 1), "dve")
    add(("slots", 1, 0), "dve")
    add(("slots", 1, 1), "dve")

    plan, drained, last_of_bank = {}, {"act": 0, "dve": 0}, {}
    for n, (name, who) in enumerate(jobs):
        drained[who] += 1
        plan[name] = dict(n=n, bank=n % BANKS, full=n + 1, who=who, drained=drained[who],
                          before=last_of_bank.get(n % BANKS))
        last_of_bank[n % BANKS] = name
    return plan


def slots_before():
    at, n = {}, 0
    for name, slots in (("mod0a", 8), ("in0", 10), ("mod", 24), ("mod12", 4), ("out0", 4), ("mod13", 4), ("mod14", 8),
                        ("moe0", 3 * EXPERTS), ("in1", 12), ("out1", 4), ("moe1", 3 * EXPERTS)):
        at[name] = n
        n += slots
    return at


EVEN_BLOCKS = [("u", 0, 6), ("g", 0, 8), ("u", 1, 7), ("g", 1, 9), ("q", 0, 0), ("q", 1, 1),
               ("k", 0, 2), ("k", 1, 3), ("v", 0, 4), ("v", 1, 5)]
ODD_BLOCKS = [("dq", 0, 6), ("dq", 1, 7), ("dk", 0, 8), ("dk", 1, 9), ("dv", 0, 10), ("dv", 1, 11),
              ("cc", 0, 2), ("cu", 0, 4), ("cb", 0, 0), ("cc", 1, 3), ("cu", 1, 5), ("cb", 1, 1)]


def trunk(nc, A):
    plan = psum_plan()
    at = slots_before()

    ctx = ExitStack()
    with ctx:
        def sb(name, shape, dt=F32):
            return ctx.enter_context(nc.sbuf_tensor(name, shape, dt))

        def sem(name):
            return ctx.enter_context(nc.semaphore(name))

        X = sb("X", [P, 4, D])
        ring = sb("ring", [P, RING, SLOT])
        RH = sb("RH", [P, 4096])
        RT = sb("RT", [P, 4096])
        RAB = sb("RAB", [P, 4096])
        G = sb("G", [P, 2, D])
        modrow = sb("modrow", [P, MOD_PER_LAYER, BLK])
        grow = sb("grow", [P, 2, BLK])
        const = sb("const", [P, C_END])
        csilu = sb("csilu", [P, NCH, 32])
        zero_one = sb("zero_one", [P, 2, P], F16)
        craw = sb("craw", [P, 2, NCH])
        WR = sb("WR", [P, NCH, GROUPS + EXPERTS])
        RB = sb("RB", [P, GROUPS + EXPERTS])
        RM = sb("RM", [P, 2288])
        BIAS = sb("BIAS", [P, 4, 6, 64])
        PR = sb("PR", [P, 2, 512])
        chan = sb("chan", [P, 4, 40])
        small = sb("small", [P, 256])
        idx = sb("idx", [P, NBLK, 2, EXPERTS], I32)
        sidx = sb("sidx_all", [P, 24], I32)
        extra_i = sb("extra_i", [1, 2, EXPERTS // PER_LOOP], I32)
        ps = ctx.enter_context(nc.psum_tensor("ps", [P, BANKS, 512], F32))

        ident = const[:, C_ID:C_ID + P]
        swap = const[:, C_SWAP:C_SWAP + P]
        reverse = const[:, C_REV:C_REV + P]
        ones = const[:, C_ONE:C_ONE + P]
        iota = const[:, C_IOTA:C_IOTA + CAP]

        H = RH[:, :].rearrange("p (t d) -> p t d", t=4)
        QK = RH[:, :].rearrange("p (f t) -> p f t", f=8)
        DQ = RH[:, 0:1024].rearrange("p (f t) -> p f t", f=4)
        DK = RH[:, 1024:3072].rearrange("p (f t) -> p f t", f=4)
        ROT = RH[:, 3072:4096].rearrange("p (b t) -> p b t", b=2)
        hT = RT[:, :].rearrange("p (c t) -> p c t", c=NCH)
        aT = RT[:, 0:2048].rearrange("p (f t) -> p f t", f=4)
        PTX = RT[:, 2048:3072].rearrange("p (k q) -> p k q", k=4)
        PTC = RT[:, 3072:3584].rearrange("p (k q) -> p k q", k=2)
        PROBS = [PR[:, 0, :], PR[:, 1, :], G[:, 1, 0:512]]
        dT = RT[:, 0:1024].rearrange("p (f t) -> p f t", f=4)
        DPT = RT[:, 2048:3072].rearrange("p (b k q) -> p b k q", b=2, k=4)
        GF = modrow[:, 0:4, :].rearrange("p v n -> p (v n)")
        chan_rows = PR[:, 0, :]
        LAMROW = PR[:, 0, 0:256]
        SCALE = RAB[:, 0:2048].rearrange("p (s d) -> p s d", s=2)
        SHIFT = RAB[:, 2048:4096].rearrange("p (s d) -> p s d", s=2)
        V = RAB[:, 0:2048].rearrange("p (t d) -> p t d", t=4)
        Y = RAB[:, 2048:4096].rearrange("p (c t) -> p c t", c=4)
        DP = RAB[:, 2048:4096].rearrange("p (n k) -> p n k", n=4)
        Z = RM[:, :].rearrange("p (c s t) -> p c s t", c=4, s=2)
        SQ = RM[:, 0:2048].rearrange("p (c t) -> p c t", c=4)
        SG = PR
        SD = PR[:, 0, :]
        CU = RM[:, 0:4 * (SEQ + 2)].rearrange("p (c t) -> p c t", c=4)
        CC = RM[:, 1032:1032 + 1024].rearrange("p (c t) -> p c t", c=4)
        BIASF = BIAS[:, :, :, :].rearrange("p h j k -> p (h j k)")
        COS, SIN = BIASF[:, 0:SEQ], BIASF[:, SEQ:2 * SEQ]
        CV = BIASF[:, 512:1536].rearrange("p (c t) -> p c t", c=4)
        OD = PR[:, :, :].rearrange("p a b -> p (a b)").rearrange("p (n d) -> p n d", n=8)
        back = [(0, 1, RT[:, 0:2048]), (0, 1, RT[:, 2048:4096]), (1, 0, RH[:, 2048:4096]), (0, 1, RM[:, 0:2048])]
        XG = RH[:, 0:2048].rearrange("p (b d) -> p b d", b=4)
        YS = RH[:, 2048:3072].rearrange("p (b d) -> p b d", b=2)
        XGX, YSX = RH[:, 3072:3584], RH[:, 3584:4096]
        XT = RT[:, 0:1024].rearrange("p (b j a s) -> p b j a s", b=2, j=4, a=2)
        XTX = RT[:, 1024:1536].rearrange("p (j a s) -> p j a s", j=4, a=2)
        SA = RT[0:CAP, 1536:2048].rearrange("p (b f) -> p b f", b=2)
        HID = RT[0:CAP, 2048:2560].rearrange("p (b f) -> p b f", b=2)
        SAX, HIDX = RT[0:CAP, 2560:2816], RT[0:CAP, 2816:3072]
        HT = RT[:, 3072:3328].rearrange("p (b f s) -> p b f s", b=2, f=2)
        HTX = RT[:, 3328:3456].rearrange("p (f s) -> p f s", f=2)
        GIDX = [sidx[:, 2 * b:2 * b + 1] for b in range(4)]
        SIDX = [sidx[:, 8 + 2 * b:9 + 2 * b] for b in range(2)]
        GIDXX, SIDXX = sidx[:, 12:13], sidx[:, 14:15]

        sumsq = small[:, 0:20].rearrange("p (k t) -> p k t", k=5)
        root = small[:, 20:40].rearrange("p (k t) -> p k t", k=5)
        rstd = small[:, 40:60].rearrange("p (k t) -> p k t", k=5)
        eps = small[:, 60:61]
        nmax = small[:, 64:96]
        m1 = small[:, 96:97]
        m2 = small[:, 97:98]
        sums = small[:, 100:108]
        rsum = small[:, 112:116]
        lam = small[:, 116:124]
        subln = small[:, 124:125]
        sublns = small[:, 125:126]
        dss = small[:, 128:136]
        droot = small[:, 136:144]
        drstd = small[:, 144:152]
        topw = small[:, 152:160].rearrange("p (t k) -> p t k", t=4)
        sumsq_parts = small[:, 176:208].rearrange("p (l t b) -> p l t b", l=2, t=4)
        def temp(at, *shape):
            n = int(np.prod(shape))
            names = "abcd"[:len(shape)]
            return RM[:, at:at + n].rearrange(f"p ({' '.join(names)}) -> p {' '.join(names)}",
                                              **{k: v for k, v in zip(names, shape)})
        logits = temp(0, 4, GROUPS + EXPERTS)
        chosen = RM[:, 144:208].bitcast(F16).rearrange("p (t e) -> p t e", t=4)
        first_choice, second_choice = temp(272, 4, EXPERTS), temp(400, 4, EXPERTS)
        masked, cand = temp(528, 4, EXPERTS), temp(656, 4, EXPERTS)
        choices, ranked = temp(272, 2, 4, EXPERTS), temp(528, 2, 4, EXPERTS)
        gcand, ghot, gpen = temp(912, 4, GROUPS), temp(928, 4, GROUPS), temp(944, 4, GROUPS)
        rarg = temp(960, 5, 4)
        rexp = temp(980, 5, 4)
        gmax, emax, emax2, least, gsum = [temp(1000 + 4 * i, 4) for i in range(5)]
        rank_of = temp(1020, 8)
        count, blocks, packed = temp(1032, EXPERTS), temp(1064, EXPERTS), temp(1096, EXPERTS)
        words = temp(1128, EXPERTS // PER_LOOP)
        at_slot = RM[:, 1136:1648].bitcast(F16).rearrange("p (b n s) -> p b n s", b=2, n=8)
        rows_of = PR[:, 1, 0:256].bitcast(F16).rearrange("p (n v e) -> p n v e", n=8, v=2)

        psum_full = sem("psum_full")
        act_drained = sem("act_drained")
        dve_drained = sem("dve_drained")
        landed = [sem(f"landed{i}") for i in range(RING)]
        ring_free = sem("ring_free")
        ld_const, ld_x, ld_c, ld_bmod, ld_rows, ld_grow, ld_router, ld_lam, ld_rot, ld_final = (
            sem(n) for n in ("ld_const", "ld_x", "ld_c", "ld_bmod", "ld_rows", "ld_grow", "ld_router",
                             "ld_lam", "ld_rot", "ld_final"))
        ld_bias = [sem(f"ld_bias{i}") for i in range(4)]
        pe_passed, pool_passed = sem("pe_passed"), sem("pool_passed")
        zeroed = sem("zeroed")
        dve_zeroed = sem("dve_zeroed")
        c_silu = sem("c_silu")
        act_step, dve_step, pool_step = sem("act_step"), sem("dve_step"), sem("pool_step")
        squares = sem("squares")
        sums_ready = sem("sums_ready")
        norm_root = sem("norm_root")
        h_scaled = sem("h_scaled")
        h_ready = [sem("h_ready_even"), sem("h_ready_odd")]
        row_scale = sem("row_scale")
        gated_in = sem("gated_in")
        z_clear = sem("z_clear")
        conv_step = sem("conv_step")
        ld_bias1 = {v: sem(f"ld_bias1_{v}") for v in range(MOD_PER_LAYER)}
        bias_ready = sem("bias_ready")
        max_ready = sem("max_ready")
        probs_ready = sem("probs_ready")
        centred = sem("centred")
        squared = sem("squared")
        ln_scaled = sem("ln_scaled")
        b_ready = sem("b_ready")
        x_updated = sem("x_updated")
        h_stored = sem("h_stored")
        router_exp = sem("router_exp")
        router_max = sem("router_max")
        one_hot = sem("one_hot")
        slot_hot = sem("slot_hot")
        slot_used = sem("slot_used")
        extra_ready = sem("extra_ready")
        gidx_ready, sidx_ready = sem("gidx_ready"), sem("sidx_ready")
        gathered = [sem(f"gathered{i}") for i in range(4)]
        scattered = [sem(f"scattered{i}") for i in range(2)]
        xT_full, xT_ready = sem("xT_full"), sem("xT_ready")
        up_full, gate_ready, hid_ready = sem("up_full"), sem("gate_ready"), sem("hid_ready")
        hidT_full, hidT_ready = sem("hidT_full"), sem("hidT_ready")
        y_full, y_ready = sem("y_full"), sem("y_ready")
        x_gidx, x_gathered, x_scattered = sem("x_gidx"), sem("x_gathered"), sem("x_scattered")
        x_xT_full, x_xT_ready = sem("x_xT_full"), sem("x_xT_ready")
        x_up_full, x_gate_ready, x_hid_ready = sem("x_up_full"), sem("x_gate_ready"), sem("x_hid_ready")
        x_hidT_full, x_hidT_ready = sem("x_hidT_full"), sem("x_hidT_ready")
        x_y_full, x_y_ready = sem("x_y_full"), sem("x_y_ready")
        pairs_stored = sem("pairs_stored")
        y_back = [sem(f"y_back{t}") for t in range(4)]
        y_scaled = sem("y_scaled")
        combined = sem("combined")
        stored = sem("stored")
        lam_sums, lam_exp, lam_ready = sem("lam_sums"), sem("lam_exp"), sem("lam_ready")
        o_squared = sem("o_squared")
        o_root = sem("o_root")
        o_scaled = sem("o_scaled")
        final_ready = sem("final_ready")
        rot_ready = sem("rot_ready")

        tiles_of = {0: 4, 1: 2}
        tokens = [P * tiles_of[l] for l in (0, 1)]
        hrow = [nc.dram_tensor(f"hrow{l}", [2 * tokens[l], 512], F32).ap() for l in (0, 1)]
        pair_out = [nc.dram_tensor(f"pair_out{l}", [4 * tokens[l], 512], F32).ap() for l in (0, 1)]

        norm_tiles = [4, 4, 4, 2, 2]
        h_before = [sum(norm_tiles[:k]) for k in range(6)]
        xu_mix = [8, 8 + 4 + 4]
        xu_moe = [8 + 4, 8 + 4 + 4 + 2]

        def h_wait(eng, k, t):
            place = TILE_ORDER[norm_tiles[k]].index(t)
            eng.wait_ge(h_ready[t % 2], (h_before[k] + place - place % 2) // 2 + 1)

        def hT_drained(eng, k):
            last = TILE_ORDER[norm_tiles[k]][-1]
            drained(eng, "hT", k, last, 0)
            drained(eng, "hT", k, last, 1)

        block = ctx.enter_context(nc.Block())

        def full(eng, *name):
            eng.wait_ge(psum_full, plan[name]["full"])
            return ps[:, plan[name]["bank"], :]

        def drained(eng, *name):
            job = plan[name]
            eng.wait_ge(act_drained if job["who"] == "act" else dve_drained, job["drained"])

        def job_after(i, q, k):
            return (i, q + k) if q + k < PER_LOOP else (i + 1, q + k - PER_LOOP)

        def extra_counts(eng, l, i):
            word = eng.value_load(extra_i[0:1, l, i:i + 1] if isinstance(i, int) else
                                  extra_i[0:1, l, bass.ds(i, 1)], min_val=0, max_val=4095)
            return [(word >> (3 * q)) & 7 for q in range(PER_LOOP)]

        def chained(eng, semaphore):
            count = [0]

            def step(ins, wait=True):
                count[0] += 1
                ins.then_inc(semaphore, 1)
                if wait:
                    eng.wait_ge(semaphore, count[0])

            step.sync = lambda: eng.wait_ge(semaphore, count[0])
            step.lag = lambda n: eng.wait_ge(semaphore, count[0] - n)
            return step

        @block.sync
        def _(sp):
            sp.dma_start(const[:, :], A["consts"]).then_inc(ld_const, 16)
            slots_filled = [0]

            def load(halves):
                n = slots_filled[0]
                if n >= RING:
                    sp.wait_ge(ring_free, n - RING + 1)
                for dst, src in halves(ring[:, n % RING, :]):
                    sp.dma_start(dst, src).then_inc(landed[n % RING], 16)
                slots_filled[0] += 1

            def columns(w, b, rows="features"):
                w = w[:, b * BLK:(b + 1) * BLK]

                def halves(slot):
                    for a in (0, 1):
                        rows_a = w[512 * a:512 * (a + 1), :]
                        yield (slot[:, 1024 * a:1024 * (a + 1)].rearrange("p (j n) -> p j n", n=BLK),
                               rows_a.rearrange("(p j) n -> p j n", j=4) if rows == "features" else
                               rows_a.rearrange("(j p) n -> p j n", p=P))

                load(halves)

            def modulation(l, vectors):
                for v in vectors:
                    for b in range(4):
                        columns(A["w_mod"][l], 4 * v + b)

            def experts(l):
                base = at[f"moe{l}"]
                assert slots_filled[0] == base
                with sp.Fori(0, EXPERTS // PER_LOOP) as i:
                    for q in range(PER_LOOP):
                        for k, name in enumerate(("moe_w1", "moe_w3", "moe_w2")):
                            n = base + 3 * q + k
                            sp.wait_ge(ring_free, i * RING + (n - RING + 1))
                            w = A[name][l, bass.ds(i * PER_LOOP + q, 1), :, :]
                            for a in (0, 1):
                                if k < 2:
                                    src = w[:, 512 * a:512 * (a + 1), :].rearrange("e (p j) n -> p (e j n)", j=4)
                                else:
                                    src = w.rearrange("e (p f) n -> p f (e n)", p=P)[:, a, :]
                                sp.dma_start(ring[:, n % RING, 1024 * a:1024 * (a + 1)],
                                             src).then_inc(landed[n % RING], 16)
                slots_filled[0] += 3 * EXPERTS

            def outputs_back(l):
                sp.wait_ge(pairs_stored, l + 1)
                for t in TILE_ORDER[tiles_of[l]]:
                    sp.dma_start(back[t][2], pair_out[l][4 * P * t:4 * P * (t + 1), :].rearrange("(p r) d -> p (r d)", r=4)
                                 ).then_inc(y_back[t], 16)

            sp.dma_start(X[:, 0:2, :], A["x"][0].rearrange("(t p) d -> p t d", p=P)).then_inc(ld_x, 16)
            sp.dma_start(X[:, 2:4, :], A["ctx"][0].rearrange("(t p) d -> p t d", p=P)).then_inc(ld_x, 16)
            modulation(0, (1, 0))
            for _, _, b in EVEN_BLOCKS:
                columns(A["even_w_in"][0], b)
            for l, v in MOD_AFTER.values():
                modulation(l, (v,))
            modulation(1, (2,))
            for b in range(4):
                columns(A["even_w_out"][0], b, rows="tiles")
            modulation(1, (3, 4, 5))
            experts(0)
            for _, _, b in ODD_BLOCKS[:3]:
                columns(A["odd_w_in"][0], b)
            outputs_back(0)
            for _, _, b in ODD_BLOCKS[3:]:
                columns(A["odd_w_in"][0], b)
            for b in range(4):
                columns(A["odd_w_out"][0], b, rows="tiles")
            experts(1)
            outputs_back(1)
            sp.wait_ge(stored, 32)

        @block.tensor
        def _(pe):
            order = iter(plan)
            used = [0]

            def open_bank(*name):
                assert next(order) == name, name
                before = plan[name]["before"]
                if before:
                    drained(pe, *before)
                return ps[:, plan[name]["bank"], :]

            def close(mm):
                mm.then_inc(psum_full, 1)

            free_due = [0]

            def free(k):
                free_due[0] += k

            def freed(mm):
                if free_due[0]:
                    mm.then_inc(ring_free, free_due[0])
                    free_due[0] = 0

            def slot(n):
                pe.wait_ge(landed[n % RING], 32 * (n // RING + 1))
                return ring[:, n % RING, :].rearrange("p (c n) -> p c n", n=BLK)

            def modulation(l, v, first):
                bank = open_bank("mod", l, v)
                pe.wait_ge(c_silu, 1)
                w = [slot(first + j) for j in range(4)]
                for c in range(NCH):
                    for j in range(4):
                        mm = pe.matmul(bank[32 * j:32 * j + 32, 0:BLK], csilu[:, c, :], w[j][:, c, :],
                                       start=(c == 0), stop=(c == NCH - 1))
                        if c == 0 and j == 0:
                            freed(mm)
                close(mm)
                free(4)

            def rows(k, what, v, streams=(LATENT, CONTEXT)):
                for s in streams:
                    for hf in (0, 1):
                        bank = open_bank("row", k, what, s, hf)
                        if what == "scale":
                            pe.wait_ge(row_scale, k + 1)
                        else:
                            drained(pe, "mod", k // 2, v)
                        for j in (2 * hf, 2 * hf + 1):
                            mm = pe.matmul(bank[:, BLK * (j % 2):BLK * (j % 2 + 1)],
                                           ident[:, 32 * j + s:32 * j + s + 1].broadcast_to([P, P]),
                                           modrow[:, v, :], start=True, stop=True)
                            freed(mm)
                        close(mm)

            def transpose_tile(k, t):
                h_wait(pe, k, t)
                for a in (0, 1):
                    bank = open_bank("hT", k, t, a)
                    for j in range(4):
                        mm = pe.transpose(bank[:, P * j:P * (j + 1)], H[:, t, 512 * a + j:512 * (a + 1):4], ident)
                        if j == 0:
                            freed(mm)
                    close(mm)

            def transposes(k):
                for t in TILE_ORDER[norm_tiles[k]]:
                    transpose_tile(k, t)

            def by_feature(bank, w, ft, moving):
                for c in range(NCH):
                    mm = pe.matmul(bank, w[:, c, P * ft:P * (ft + 1)], moving[:, c, :],
                                   start=(c == 0), stop=(c == NCH - 1))
                    if c == 0:
                        freed(mm)
                return mm

            def by_token(bank, w, tiles, chunk_of):
                for i, t in enumerate(tiles):
                    for c in range(NCH):
                        mm = pe.matmul(bank[:, BLK * i:BLK * (i + 1)], chunk_of(c, t), w[:, c, :],
                                       start=(c == 0), stop=(c == NCH - 1))
                        if c == 0:
                            freed(mm)
                return mm

            def transposes_and_router(l):
                k, T = 1 + 2 * l, tiles_of[l]
                bank = ps[:, plan["logit", l]["bank"], :]

                def logits_of(t, first):
                    for a in (0, 1):
                        drained(pe, "hT", k, t, a)
                    if first:
                        drained(pe, *plan["logit", l]["before"])
                        pe.wait_ge(ld_router, 16 * 6 * (l + 1))
                    for c in range(NCH):
                        mm = pe.matmul(bank[:, 36 * t:36 * t + 36], hT[:, c, P * t:P * (t + 1)], WR[:, c, :],
                                       start=(c == 0), stop=(c == NCH - 1))
                    return mm

                tiles = TILE_ORDER[T]
                for i, t in enumerate(tiles):
                    transpose_tile(k, t)
                    if i >= 1:
                        logits_of(tiles[i - 1], i == 1)
                open_bank("logit", l)
                close(logits_of(tiles[-1], False))

            def ranks(l):
                T = tiles_of[l]
                bank = open_bank("rank", l)
                pe.wait_ge(one_hot, l + 1)
                M, tri, every = chosen, zero_one[:, 0, :], zero_one[:, 1, :]
                for t in range(T):
                    out = bank[:, EXPERTS * t:EXPERTS * (t + 1)]
                    for u in range(t):
                        pe.matmul(out, every, M[:, u, :], start=(u == 0), stop=False)
                    mm = pe.matmul(out, tri, M[:, t, :], start=(t == 0), stop=True)
                for t in range(T):
                    mm = pe.matmul(bank[:, EXPERTS * 4:EXPERTS * 5], every, M[:, t, :],
                                   start=(t == 0), stop=(t == T - 1))
                close(mm)

            def slot_rows(l, part):
                T = tiles_of[l]
                n_blocks = T * P // CAP
                bank = open_bank("slots", l, part)
                for b in range(1, n_blocks) if part else (0,):
                    pe.wait_ge(slot_hot, (0, NBLK)[l] + b + 1)
                    out = bank[:, 2 * EXPERTS * (b - part):2 * EXPERTS * (b - part + 1)]
                    for n in range(2 * T):
                        for half in (0, 1):
                            mm = pe.matmul(out[CAP * half:CAP * (half + 1), :], at_slot[:, b % 2, n, :],
                                           rows_of[:, n, :, :].rearrange("p v e -> p (v e)"),
                                           start=(n == 0), stop=(n == 2 * T - 1))
                    if 0 < b < n_blocks - 1:
                        mm.then_inc(slot_used, 1)
                close(mm)

            extras = pe.alloc_register("pe_extras")
            pe.reg_mov(extras, 0)

            def experts(l):
                n0, base = EXPERTS * l, at[f"moe{l}"]
                end = plan["slots", l, 1]["n"]
                for name in list(plan)[end - BANKS + 1:end + 1]:
                    drained(pe, *name)

                def T(i, q, start=False):
                    n, b = i * PER_LOOP + (n0 + q), q % 2
                    pe.wait_ge(gathered[q % 4], (i + ((n0 + q) // 4 + 1)) * 16)
                    if not start:
                        pe.wait_ge(xT_ready, n - 1)
                    for j in range(4):
                        mm = pe.transpose(ps[:, b, P * j:P * (j + 1)], XG[:, q % 4, j:512:4], ident)
                        if j == 0:
                            freed(mm)
                    mm.then_inc(xT_full, 1)

                def wait_slot(i, q, k):
                    s = base + 3 * q + k
                    pe.wait_ge(landed[s % RING], (i + (s // RING + 1)) * 32)
                    return ring[:, s % RING, :]

                def U(i, q, start=False):
                    n, b = i * PER_LOOP + (n0 + q), q % 2
                    pe.wait_ge(xT_ready, n + 1)
                    if not start:
                        pe.wait_ge(hid_ready, n - 1)
                    w = [wait_slot(i, q, k) for k in (0, 1)]
                    up(w, lambda c: XT[:, b, c % 4, c // 4, :], ps[:, 2 + b, :]).then_inc(up_full, 1)

                def up(w, xt, bank):
                    for c in range(NCH):
                        for k in (0, 1):
                            mm = pe.matmul(bank[CAP * k:CAP * (k + 1), 0:BLK], xt(c),
                                           w[k][:, BLK * c:BLK * (c + 1)], start=(c == 0), stop=(c == NCH - 1))
                    return mm

                def Hd(i, q):
                    n, b = i * PER_LOOP + (n0 + q), q % 2
                    pe.wait_ge(hid_ready, n + 1)
                    pe.sem_inc(pe_passed, 1)
                    for f in (0, 1):
                        mm = pe.transpose(ps[:, 4, 128 * b + CAP * f:128 * b + CAP * (f + 1)],
                                          HID[:, b, f:BLK:2], ident[0:CAP, 0:CAP])
                        if f == 0:
                            freed(mm)
                    mm.then_inc(hidT_full, 1)

                def Dn(i, q):
                    n, b = i * PER_LOOP + (n0 + q), q % 2
                    pe.wait_ge(hidT_ready, n + 1)
                    w = wait_slot(i, q, 2)
                    down(w, lambda f: HT[:, b, f, :], ps[:, 5 + b, :]).then_inc(y_full, 1)

                def down(w, ht, bank):
                    for f in (0, 1):
                        for k in (0, 1):
                            mm = pe.matmul(bank[CAP * k:CAP * (k + 1), :], ht(f),
                                           w[:, D * f + 512 * k:D * f + 512 * (k + 1)],
                                           start=(f == 0), stop=(f == 1))
                    return mm

                def more(q, count):
                    w = [ring[:, (base + 3 * q + k) % RING, :] for k in range(3)]
                    bank = ps[:, 7, :]
                    with pe.If(count > 0):
                        with pe.Fori(0, count):
                            pe.wait_ge(x_y_ready, pe.snap(extras))
                            pe.reg_add(extras, extras, 1)
                            x = pe.snap(extras)
                            pe.wait_ge(x_gathered, x * 16)
                            for j in range(4):
                                mm = pe.transpose(bank[:, P * j:P * (j + 1)], XGX[:, j:512:4], ident)
                            mm.then_inc(x_xT_full, 1)
                            pe.wait_ge(x_xT_ready, x)
                            up(w, lambda c: XTX[:, c % 4, c // 4, :], bank).then_inc(x_up_full, 1)
                            pe.wait_ge(x_hid_ready, x)
                            pe.sem_inc(pe_passed, 1)
                            for f in (0, 1):
                                mm = pe.transpose(bank[:, CAP * f:CAP * (f + 1)], HIDX[:, f:BLK:2],
                                                  ident[0:CAP, 0:CAP])
                            mm.then_inc(x_hidT_full, 1)
                            pe.wait_ge(x_hidT_ready, x)
                            down(w[2], lambda f: HTX[:, f, :], bank).then_inc(x_y_full, 1)

                def step(i, q, count, ahead2=True, ahead1=True):
                    if ahead2:
                        T(*job_after(i, q, 2))
                    Hd(i, q)
                    if ahead1:
                        U(*job_after(i, q, 1))
                    Dn(i, q)
                    more(q, count)
                    free(3)

                T(0, 0, start=(l == 0))
                T(0, 1, start=(l == 0))
                U(0, 0, start=(l == 0))
                pe.wait_ge(extra_ready, l + 1)

                last = EXPERTS // PER_LOOP - 1
                c = extra_counts(pe, l, 0)
                for q in range(PER_LOOP):
                    step(0, q, c[q])
                with pe.Fori(1, last) as i:
                    c = extra_counts(pe, l, i)
                    for q in range(PER_LOOP):
                        step(i, q, c[q])
                c = extra_counts(pe, l, last)
                for q in range(PER_LOOP):
                    step(last, q, c[q], ahead2=(q < 2), ahead1=(q < 3))
                pe.wait_ge(y_ready, n0 + EXPERTS)
                pe.wait_ge(x_y_ready, pe.snap(extras))

            pe.wait_ge(ld_const, 16)
            bank = open_bank("chan")
            pe.wait_ge(ld_rows, 16 * 5)
            for c in range(4):
                mm = pe.transpose(bank[:, 40 * c:40 * c + 37], chan_rows[0:37, P * c:P * (c + 1)], ident[0:37, 0:37])
            close(mm)
            n = at["mod0a"]
            modulation(0, 1, n)
            rows(0, "scale", 1)
            modulation(0, 0, n + 4)
            rows(0, "shift", 0)
            transposes(0)
            hT_drained(pe, 0)
            def scores(n):
                h, qt = n // 4, n % 4
                ft, p0 = h // 2, A_DIM * (h % 2)
                bank = open_bank("S", n)
                drained(pe, "q", ft // 2, ft % 2)
                drained(pe, "k", ft // 2, ft % 2)
                k0 = 0 if qt < 2 else SEQ
                mm = pe.matmul(bank[:, k0:TOK], QK[p0:p0 + A_DIM, ft, P * qt:P * (qt + 1)],
                               QK[p0:p0 + A_DIM, 4 + ft, k0:TOK], start=True, stop=(qt >= 2),
                               skip_group_check=(qt < 2))
                if qt < 2:
                    pe.wait_ge(bias_ready, h + 1)
                    start = (2 - 2 * qt) * GRID_W
                    bias = BIAS[:, h % 4, :, :].rearrange("p j k -> p (j k)")[:, start:start + SEQ]
                    mm = pe.matmul(bank[:, 0:SEQ], reverse, bias, start=False, stop=True, skip_group_check=True)
                close(mm)

            for i, (what, b, _) in enumerate(EVEN_BLOCKS):
                if (what, b) == ("v", 0):
                    for n in range(S_AHEAD):
                        scores(n)
                w = slot(at["in0"] + i)
                if what == "v":
                    for tp in (0, 1):
                        bank = open_bank(what, b, tp)
                        close(by_token(bank, w, (2 * tp, 2 * tp + 1), lambda c, t: hT[:, c, P * t:P * (t + 1)]))
                else:
                    for ft in (0, 1):
                        bank = open_bank(what, b, ft)
                        close(by_feature(bank, w, ft, hT))
                free(1)

            def probs_T(n):
                qt = n % 4
                bank = open_bank("PT", n)
                pe.wait_ge(probs_ready, n + 1)
                for kt in range(0 if qt < 2 else 2, 4):
                    mm = pe.transpose(bank[:, P * kt:P * (kt + 1)], PROBS[n % S_AHEAD][:, P * kt:P * (kt + 1)], ident)
                    if kt == 2:
                        freed(mm)
                close(mm)

            def weighted(h):
                p0 = A_DIM * (h % 2)
                bank = open_bank("O", h)
                for n in range(4 * h, 4 * h + 4):
                    drained(pe, "PT", n)
                if h == 0:
                    for tp in (0, 1):
                        drained(pe, "v", 1, tp)
                for kt in range(4):
                    mm = pe.matmul(bank[p0:p0 + A_DIM, 0:SEQ], V[:, kt, A_DIM * h:A_DIM * (h + 1)], PTX[:, kt, :],
                                   start=(kt == 0), stop=(kt == 3))
                for kt in (2, 3):
                    mm = pe.matmul(bank[p0:p0 + A_DIM, SEQ:TOK], V[:, kt, A_DIM * h:A_DIM * (h + 1)],
                                   PTC[:, kt - 2, :], start=(kt == 2), stop=(kt == 3))
                close(mm)

            units = 4 * A_HEADS
            for n in range(units):
                probs_T(n)
                if n % 4 == 0 and n:
                    weighted(n // 4 - 1)
                if n + S_AHEAD < units:
                    scores(n + S_AHEAD)
                if n in MOD_AFTER:
                    modulation(*MOD_AFTER[n], at["mod"] + 4 * (n // 5))
            weighted(A_HEADS - 1)

            bank = open_bank("mean")
            pe.wait_ge(conv_step, 4 * TAPS)
            for ct in range(4):
                mm = pe.matmul(bank, ones, Y[:, ct, :], start=(ct == 0), stop=(ct == 3))
            close(mm)
            rows(0, "gate", 2)
            modulation(1, 2, at["mod12"])
            bank = open_bank("var")
            for ct in range(4):
                pe.wait_ge(squared, ct + 1)
                mm = pe.matmul(bank, ones, SQ[:, ct, :], start=(ct == 0), stop=(ct == 3))
            close(mm)
            drained(pe, "O", A_HEADS - 1)
            for b in range(4):
                w = slot(at["out0"] + b)
                banks = [open_bank("out", 0, b, tp) for tp in (0, 1)]
                for source, chunks in ((aT, range(4)), (Y, range(4, NCH))):
                    if source is Y:
                        pe.wait_ge(b_ready, 4)
                    for t in range(4):
                        out = banks[t // 2][:, BLK * (t % 2):BLK * (t % 2 + 1)]
                        for c in chunks:
                            mm = pe.matmul(out, source[:, c % 4, P * t:P * (t + 1)], w[:, c, :],
                                           start=(c == 0 and t % 2 == 0), stop=(c == NCH - 1), skip_group_check=True)
                            if c == 0:
                                freed(mm)
                        if source is Y and t % 2:
                            close(mm)
                free(1)
            rows(1, "scale", 4)
            rows(1, "shift", 3)
            rows(1, "gate", 5)
            modulation(1, 3, at["mod13"])
            modulation(1, 4, at["mod14"])
            transposes_and_router(0)
            modulation(1, 5, at["mod14"] + 4)
            ranks(0)
            slot_rows(0, 0)
            slot_rows(0, 1)
            experts(0)

            rows(2, "scale", 1)
            rows(2, "shift", 0)
            transposes(2)
            hT_drained(pe, 2)
            def diff_scores(n):
                h, qt = n // 2, n % 2
                if qt == 0:
                    pe.wait_ge(rot_ready, 4 + h + 1)
                for m in (0, 1):
                    bank = open_bank("DS", n, m)
                    mm = pe.matmul(bank, DQ[64 * m:64 * m + 64, h, P * qt:P * (qt + 1)],
                                   DK[64 * m:64 * m + 64, h, :], start=True, stop=True)
                    close(mm)

            for i, (what, b, _) in enumerate(ODD_BLOCKS):
                if (what, b) == ("cc", 0):
                    diff_scores(0)
                    diff_scores(1)
                w = slot(at["in1"] + i)
                if what == "dv":
                    for tp in (0, 1):
                        bank = open_bank(what, b, tp)
                        close(by_token(bank, w, (2 * tp, 2 * tp + 1), lambda c, t: hT[:, c, P * t:P * (t + 1)]))
                elif what in ("dq", "dk"):
                    tok = SEQ if what == "dq" else TOK
                    for ft in (0, 1):
                        bank = open_bank(what, b, ft)
                        close(by_feature(bank[:, 0:tok], w, ft, hT[:, :, 0:tok]))
                        bank = open_bank(what + "swap", b, ft)
                        drained(pe, what, b, ft)
                        src = (DQ if what == "dq" else DK)[:, 2 * b + ft, 0:SEQ]
                        close(pe.matmul(bank[:, 0:SEQ], swap, src, start=True, stop=True))
                else:
                    bank = open_bank(what, b)
                    for ft in (0, 1):
                        mm = by_feature(bank[:, SEQ * ft:SEQ * (ft + 1)], w, ft, hT[:, :, 0:SEQ])
                    close(mm)
                free(1)

            def diff_probs_T(n):
                bank = open_bank("DPT", n)
                pe.wait_ge(probs_ready, units + n + 1)
                for kt in range(4):
                    mm = pe.transpose(bank[:, P * kt:P * (kt + 1)], DP[:, 2 * (n % 2), P * kt:P * (kt + 1)], ident)
                close(mm)

            def diff_weighted(n):
                bank = open_bank("DO", n)
                drained(pe, "DPT", n)
                if n == 0:
                    drained(pe, "dv", 1, 1)
                for kt in range(4):
                    mm = pe.matmul(bank[:, 0:P], DPT[:, n % 2, kt, :], V[:, kt, P * (n // 2):P * (n // 2 + 1)],
                                   start=(kt == 0), stop=(kt == 3))
                close(mm)

            for n in range(2 * D_HEADS):
                diff_probs_T(n)
                if n + 2 < 2 * D_HEADS:
                    diff_scores(n + 2)
                if n >= 1:
                    diff_weighted(n - 1)
            diff_weighted(2 * D_HEADS - 1)
            rows(2, "gate", 2, (LATENT,))
            for n in range(2 * D_HEADS):
                bank = open_bank("DT", n)
                pe.wait_ge(o_scaled, n + 1)
                close(pe.transpose(bank[:, 0:P], OD[:, n, :], ident))
            drained(pe, "DT", 2 * D_HEADS - 1)
            drained(pe, "cb", 0)
            drained(pe, "cb", 1)
            for b in range(4):
                w = slot(at["out1"] + b)
                bank = open_bank("out", 1, b, 0)
                close(by_token(bank, w, (0, 1), lambda c, t: (CV if c < 4 else dT)[:, c % 4, P * t:P * (t + 1)]))
                free(1)
            rows(3, "scale", 4, (LATENT,))
            rows(3, "shift", 3, (LATENT,))
            transposes_and_router(1)
            rows(3, "gate", 5, (LATENT,))
            ranks(1)
            slot_rows(1, 0)
            slot_rows(1, 1)
            experts(1)

        @block.scalar
        def _(act):
            step = chained(act, act_step)

            def drain(out, bank, func=ACT.Copy, **kw):
                act.activation(out, bank, func, **kw).then_inc(act_drained, 1)

            for s, name in ((LATENT, "c"), (CONTEXT, "c_ctx")):
                src = A[name][0] if name == "c" else A[name]
                for a in (0, 1):
                    act.dma_start(craw[:, s, 4 * a:4 * a + 4],
                                  src[512 * a:512 * (a + 1)].rearrange("(p j) -> p j", j=4)).then_inc(ld_c, 16)
            at_row = 0
            for name, n in (("even_dw", TAPS), ("even_dw_b", 1), ("even_ln_g", 1), ("even_ln_b", 1), ("odd_conv", 3)):
                src = A[name][0] if n > 1 else A[name]
                act.dma_start(chan_rows[at_row:at_row + n, :], src).then_inc(ld_rows, 16)
                at_row += n

            def bias_row(v):
                bias = A["b_mod"][1].rearrange("(v j n) -> v j n", j=4, n=BLK)
                for s in (LATENT, CONTEXT):
                    act.dma_start(modrow[s:P:32, v, :], bias[v]).then_inc(ld_bias1[v], 16)
                    if v in (1, 4):
                        name = "norm_mix" if v == 1 else "norm_ffn"
                        act.dma_start(grow[s:P:32, v // 4, :],
                                      A[name][1].rearrange("(j n) -> j n", n=BLK)).then_inc(ld_bias1[v], 16)

            def router_weights(l):
                for a in (0, 1):
                    half = slice(512 * a, 512 * (a + 1))
                    act.dma_start(WR[:, 4 * a:4 * a + 4, 0:GROUPS],
                                  A["moe_wg"][l, half, :].rearrange("(p j) n -> p j n", j=4)).then_inc(ld_router, 16)
                    act.dma_start(WR[:, 4 * a:4 * a + 4, GROUPS:],
                                  A["moe_we"][l, half, :].rearrange("(p j) n -> p j n", j=4)).then_inc(ld_router, 16)
                act.dma_start(RB[:, 0:GROUPS], A["moe_bg"][l:l + 1, :].broadcast_to([P, GROUPS])).then_inc(ld_router, 16)
                act.dma_start(RB[:, GROUPS:], A["moe_be"][l:l + 1, :].broadcast_to([P, EXPERTS])).then_inc(ld_router, 16)

            def position_bias(h):
                rpb = A["even_rpb"]
                rows, cols = rpb.shape[2:]
                for half, row in ((0, 5), (1, 4)):
                    src = bass.AP(rpb.tensor, (h * rows + row) * cols + WIN_COLS - GRID_W,
                                  [[1, GRID_W], [cols, 6], [1, GRID_W]])
                    act.dma_start(BIAS[64 * half:64 * half + 64, h % 4, :, :], src).then_inc(ld_bias[h % 4], 16)

            act.wait_ge(zeroed, 1)
            for s in (LATENT, CONTEXT):
                act.dma_start(modrow[s:P:32, :, :],
                              A["b_mod"][0].rearrange("(v j n) -> j v n", j=4, n=BLK)).then_inc(ld_bmod, 16)
                for k, name in enumerate(("norm_mix", "norm_ffn")):
                    act.dma_start(grow[s:P:32, k, :], A[name][0].rearrange("(j n) -> j n", n=BLK)).then_inc(ld_bmod, 16)
            act.wait_ge(ld_c, 64)
            act.wait_ge(dve_zeroed, 1)
            act.activation(csilu[:, :, 0:2], craw[:, :, :].rearrange("p s c -> p c s"), ACT.Silu).then_inc(c_silu, 1)
            for h in range(4):
                position_bias(h)
            router_weights(0)
            act.dma_start(subln, A["odd_subln"].rearrange("o p -> p o")).then_inc(ld_lam, 16)

            tables_loaded = [0]

            def table(func):
                n = tables_loaded[0]
                act.activation(small[:, 160 + n:161 + n], eps, func)
                tables_loaded[0] += 1

            def norm_tile(k, i):
                T = norm_tiles[k]
                t = TILE_ORDER[T][i]
                if k == 0:
                    act.wait_ge(ld_x, 32)
                else:
                    act.wait_ge(x_updated, xu_moe[k // 2 - 1] - (T - 1 - i))
                junk = back[t][2][:, D * back[t][1]:D * (back[t][1] + 1)] if k in (2, 4) else H[:, t, :]
                step(act.activation(junk, X[:, t, :], ACT.Square, accum_out=sumsq[:, k, t:t + 1]))
                act.activation(root[:, k, t:t + 1], sumsq[:, k, t:t + 1], ACT.Sqrt,
                               scale=1.0 / D, bias=eps).then_inc(norm_root, 1)

            def norm_of_blocks(l):
                T = tiles_of[l]
                for b in range(4):
                    for tp in range(T // 2):
                        act.wait_ge(x_updated, xu_mix[l] - (T // 2) * 4 + b * (T // 2) + tp + 1)
                        for t in (2 * tp, 2 * tp + 1):
                            cols = slice(BLK * b, BLK * (b + 1))
                            act.activation(H[:, t, cols], X[:, t, cols], ACT.Square,
                                           accum_out=sumsq_parts[:, l, t, b:b + 1]).then_inc(squares, 1)
                act.wait_ge(sums_ready, l + 1)
                for t in TILE_ORDER[T]:
                    act.activation(root[:, 1 + 2 * l, t:t + 1], sumsq[:, 1 + 2 * l, t:t + 1], ACT.Sqrt,
                                   scale=1.0 / D, bias=eps).then_inc(norm_root, 1)

            def norm(k):
                for i in range(norm_tiles[k]):
                    norm_tile(k, i)

            def combine_and_norm(l):
                T = tiles_of[l]
                table(ACT.Sqrt)
                for i, t in enumerate(TILE_ORDER[T]):
                    first, _, y = back[t]
                    act.wait_ge(y_back[t], 16 * (l + 1))
                    y = y[:, D * first:D * (first + 1)]
                    act.activation(y, y, ACT.Identity, scale=topw[:, t, first:first + 1]).then_inc(y_scaled, 1)
                    if i >= 1 and i < T - 1 or T == 2 and i == 1:
                        norm_tile(2 * l + 2, i - 1)
                for i in range(max(T - 2, 1), T):
                    norm_tile(2 * l + 2, i)

            def shift_rows(k, streams=(LATENT, CONTEXT)):
                for s in streams:
                    for hf in (0, 1):
                        drain(SHIFT[:, s, 512 * hf:512 * (hf + 1)], full(act, "row", k, "shift", s, hf))

            def gate_rows(k, streams=(LATENT, CONTEXT)):
                for s in streams:
                    for hf in (0, 1):
                        drain(G[:, s, 512 * hf:512 * (hf + 1)], full(act, "row", k, "gate", s, hf))

            def transposed(k, store=None):
                for t in TILE_ORDER[norm_tiles[k]]:
                    if store is not None:
                        h_wait(act, k, t)
                        act.dma_start(hrow[store][2 * P * t:2 * P * (t + 1), :].rearrange("(p r) d -> p (r d)", r=2),
                                      H[:, t, :]).then_inc(h_stored, 16)
                    bank = full(act, "hT", k, t, 1)
                    drain(hT[:, 4:8, P * t:P * (t + 1)], bank.rearrange("p (j t) -> p j t", j=4))

            def router_exps(l):
                act.wait_ge(router_max, l + 1)
                act.activation(rexp[:, :, :], rarg[:, :, :], ACT.Exp).then_inc(router_exp, 1)

            extras = act.alloc_register("act_extras")
            act.reg_mov(extras, 0)

            def experts(l):
                n0 = EXPERTS * l

                def copy_xT(i, q):
                    n, b = i * PER_LOOP + (n0 + q), q % 2
                    act.wait_ge(xT_full, n + 1)
                    act.activation(XT[:, b, :, :, :].rearrange("p j a s -> p (j a s)"), ps[:, b, :],
                                   ACT.Copy).then_inc(xT_ready, 1)

                def silu(i, q):
                    n, b = i * PER_LOOP + (n0 + q), q % 2
                    act.wait_ge(up_full, n + 1)
                    act.activation(SA[:, b, :], ps[0:CAP, 2 + b, 0:BLK], ACT.Silu).then_inc(gate_ready, 1)

                def copy_y(i, q):
                    n, b = i * PER_LOOP + (n0 + q), q % 2
                    act.wait_ge(y_full, n + 1)
                    act.wait_ge(scattered[b], (i * 2 + (n0 + q) // 2) * 16)
                    act.activation(YS[:, b, :], ps[:, 5 + b, :], ACT.Copy).then_inc(y_ready, 1)

                def more(q, count):
                    bank = ps[:, 7, :]
                    with act.If(count > 0):
                        with act.Fori(0, count):
                            act.reg_add(extras, extras, 1)
                            x = act.snap(extras)
                            act.wait_ge(x_xT_full, x)
                            act.activation(XTX.rearrange("p j a s -> p (j a s)"), bank, ACT.Copy).then_inc(x_xT_ready, 1)
                            act.wait_ge(x_up_full, x)
                            act.activation(SAX, bank[0:CAP, 0:BLK], ACT.Silu).then_inc(x_gate_ready, 1)
                            act.wait_ge(x_y_full, x)
                            act.activation(YSX, bank, ACT.Copy).then_inc(x_y_ready, 1)

                def one(i, q, count, ahead2=True, ahead1=True):
                    if ahead2:
                        copy_xT(*job_after(i, q, 2))
                    if ahead1:
                        silu(*job_after(i, q, 1))
                    copy_y(i, q)
                    more(q, count)

                copy_xT(0, 0)
                copy_xT(0, 1)
                silu(0, 0)
                act.wait_ge(extra_ready, l + 1)
                last = EXPERTS // PER_LOOP - 1
                with act.Fori(0, last) as i:
                    c = extra_counts(act, l, i)
                    for q in range(PER_LOOP):
                        one(i, q, c[q])
                c = extra_counts(act, l, last)
                for q in range(PER_LOOP):
                    one(last, q, c[q], ahead2=(q < 2), ahead1=(q < 3))

            norm(0)
            shift_rows(0)
            transposed(0)
            act.wait_ge(z_clear, 1)
            def exps(n):
                act.wait_ge(max_ready, n + 1)
                bank = ps[:, plan["S", n]["bank"], :]
                keys = slice(0 if n % 4 < 2 else SEQ, TOK)
                drain(PROBS[n % S_AHEAD][:, keys], bank[:, keys], ACT.Exp, bias=nmax[:, n:n + 1],
                      accum_out=sums[:, n % 4:n % 4 + 1])
                if n % 4 == 1 and n // 4 + 4 < A_HEADS:
                    position_bias(n // 4 + 4)

            for what, b, _ in EVEN_BLOCKS:
                if (what, b) == ("v", 0):
                    act.wait_ge(gated_in, 4)
                    for n in range(S_AHEAD):
                        exps(n)
                for f in (0, 1):
                    if what == "u":
                        bank = full(act, what, b, f)
                        drain(Z[:, 2 * b + f, :, PAD:PAD + SEQ], bank.rearrange("p (s t) -> p s t", s=2))
                    elif what == "g":
                        ct = 2 * b + f
                        bank = full(act, what, b, f)
                        if ct >= 2:
                            act.wait_ge(gated_in, ct - 1)
                        drain(SG[:, ct % 2, :], bank, ACT.Sigmoid)
                    elif what == "q":
                        drain(QK[:, 2 * b + f, :], full(act, what, b, f), scale=A_DIM ** -0.5)
                    elif what == "k":
                        drain(QK[:, 4 + 2 * b + f, :], full(act, what, b, f))
                    else:
                        bank = full(act, what, b, f)
                        drain(V[:, 2 * f:2 * f + 2, BLK * b:BLK * (b + 1)], bank.rearrange("p (t n) -> p t n", t=2))

            def head_output(h):
                p0 = A_DIM * (h % 2)
                drain(aT[p0:p0 + A_DIM, h // 2, :], full(act, "O", h)[p0:p0 + A_DIM, :])

            units = 4 * A_HEADS
            bias_row(0)
            bias_row(1)
            for n in range(units):
                h, qt = n // 4, n % 4
                bank = full(act, "PT", n)
                if qt == 0 and h >= 1:
                    full(act, "O", h - 1)
                if qt < 2:
                    drain(PTX[:, :, P * qt:P * (qt + 1)], bank.rearrange("p (k q) -> p k q", k=4))
                else:
                    drain(PTC[:, :, P * (qt - 2):P * (qt - 1)], bank[:, SEQ:TOK].rearrange("p (k q) -> p k q", k=2))
                if qt == 0 and h >= 1:
                    head_output(h - 1)
                if n + S_AHEAD < units:
                    exps(n + S_AHEAD)
            head_output(A_HEADS - 1)
            gate_rows(0)
            bias_row(2)
            for ct in range(4):
                act.wait_ge(centred, ct + 1)
                act.activation(SQ[:, ct, :], Y[:, ct, :], ACT.Square).then_inc(squared, 1)
            drain(SD, full(act, "var"), ACT.Sqrt, scale=1.0 / 512, bias=eps)
            for ct in range(4):
                act.wait_ge(ln_scaled, ct + 1)
                act.activation(Y[:, ct, :], Y[:, ct, :], ACT.Silu, scale=chan[:, ct, 32:33],
                               bias=chan[:, ct, 33:34]).then_inc(b_ready, 1)
            table(ACT.Sqrt)
            norm_of_blocks(0)
            shift_rows(1)
            bias_row(3)
            bias_row(4)
            drained(act, "out", 0, 3, 1)
            gate_rows(1)
            bias_row(5)
            transposed(1, store=0)
            router_exps(0)
            drained(act, "logit", 0)
            router_weights(1)
            act.dma_start(BIASF[:, 0:512], A["rotary"]).then_inc(ld_rot, 16)
            act.dma_start(LAMROW, A["odd_lambda"].rearrange("o a b -> o (a b)").broadcast_to([P, 256])).then_inc(ld_lam, 16)
            act.wait_ge(lam_sums, 1)
            act.activation(lam[:, 2:4], lam[:, 0:2], ACT.Exp).then_inc(lam_exp, 1)
            experts(0)


            shift_rows(2)
            combine_and_norm(0)
            transposed(2)
            def diff_exps(n):
                act.wait_ge(max_ready, units + n + 1)
                for m in (0, 1):
                    drain(DP[:, 2 * (n % 2) + m, :], ps[:, plan["DS", n, m]["bank"], :], ACT.Exp,
                          bias=nmax[:, 2 * n + m:2 * n + m + 1], accum_out=sums[:, 2 * (n % 4) + m:2 * (n % 4) + m + 1])

            for what, b, _ in ODD_BLOCKS:
                if (what, b) == ("cc", 0):
                    diff_exps(0)
                    diff_exps(1)
                if what in ("cu", "cb"):
                    continue
                if what == "cc":
                    drain(CC[:, 2 * b:2 * b + 2, :], full(act, what, b).rearrange("p (c t) -> p c t", c=2))
                    continue
                for f in (0, 1):
                    bank = full(act, what, b, f)
                    if what == "dq":
                        drain(DQ[:, 2 * b + f, :], bank[:, 0:SEQ], scale=64 ** -0.5)
                    elif what == "dk":
                        drain(DK[:, 2 * b + f, :], bank)
                    else:
                        drain(V[:, 2 * f:2 * f + 2, BLK * b:BLK * (b + 1)], bank.rearrange("p (t n) -> p t n", t=2))

            for n in range(2 * D_HEADS):
                bank = full(act, "DPT", n)
                if n >= 2:
                    full(act, "DO", n - 2)
                drain(DPT[:, n % 2, :, :], bank.rearrange("p (k q) -> p k q", k=4))
                if n + 2 < 2 * D_HEADS:
                    diff_exps(n + 2)
            table(ACT.Sqrt)
            gate_rows(2, (LATENT,))
            act.wait_ge(o_squared, 2 * D_HEADS)
            act.activation(droot, dss, ACT.Sqrt, scale=1.0 / P, bias=eps).then_inc(o_root, 1)
            for n in range(2 * D_HEADS):
                h, qt = n // 2, n % 2
                drain(dT[:, h, P * qt:P * (qt + 1)], full(act, "DT", n)[:, 0:P], ACT.Identity, scale=sublns)
            norm_of_blocks(1)
            shift_rows(3, (LATENT,))
            transposed(3, store=1)
            router_exps(1)
            drained(act, "out", 1, 3, 0)
            gate_rows(3, (LATENT,))
            act.dma_start(GF, A["norm_final"].rearrange("(o d) -> o d", o=1).broadcast_to([P, D])).then_inc(ld_final, 16)
            experts(1)
            combine_and_norm(1)
            for i, t in enumerate(TILE_ORDER[2]):
                act.wait_ge(final_ready, i + 1)
                act.dma_start(A["out"][0, P * t:P * (t + 1), :], H[:, t, :]).then_inc(stored, 16)

        @block.vector
        def _(dve):
            step = chained(dve, dve_step)

            def done(ins):
                ins.then_inc(dve_drained, 1)

            step(dve.memset(eps, EPS))
            dve.memset(csilu[:, :, :], 0.0).then_inc(dve_zeroed, 1)
            dve.wait_ge(ld_const, 16)
            step(dve.tensor_copy(zero_one[:, 0, :], const[:, C_TRI:C_TRI + P]), wait=False)
            step(dve.tensor_copy(zero_one[:, 1, :], ones))
            bank = full(dve, "chan")[:, 0:160].rearrange("p (c k) -> p c k", c=4)
            done(dve.tensor_copy(chan[:, :, 0:37], bank[:, :, 0:37]))

            def modulation(l, v):
                bank = full(dve, "mod", l, v)
                if l == 0:
                    dve.wait_ge(ld_bmod, 96)
                else:
                    dve.wait_ge(ld_bias1[v], 64 if v in (1, 4) else 32)
                done(dve.tensor_tensor(modrow[:, v, :], bank[:, 0:BLK], modrow[:, v, :], ALU.add))
                if v in (1, 4):
                    drained(dve, "mod", l, v)
                    dve.scalar_tensor_tensor(out=modrow[:, v, :], in0=modrow[:, v, :], scalar=1.0,
                                             in1=grow[:, v // 4, :], op0=ALU.add, op1=ALU.mult).then_inc(row_scale, 1)

            def scale_rows(k, streams=(LATENT, CONTEXT)):
                for s in streams:
                    for hf in (0, 1):
                        done(dve.tensor_copy(SCALE[:, s, 512 * hf:512 * (hf + 1)], full(dve, "row", k, "scale", s, hf)))

            def scale_tile(k, i):
                t = TILE_ORDER[norm_tiles[k]][i]
                dve.wait_ge(norm_root, h_before[k] + i + 1)
                step(dve.reciprocal(rstd[:, k, t:t + 1], root[:, k, t:t + 1]))
                if k < 4:
                    drained(dve, "row", k, "scale", t // 2, 1)
                else:
                    dve.wait_ge(ld_final, 16)
                if k == 2 and t == 3:
                    dve.wait_ge(y_scaled, 4)
                g = SCALE[:, t // 2, :] if k < 4 else GF
                ins = dve.scalar_tensor_tensor(out=H[:, t, :], in0=X[:, t, :], scalar=rstd[:, k, t:t + 1], in1=g,
                                               op0=ALU.mult, op1=ALU.mult)
                if k == 4:
                    ins.then_inc(final_ready, 1)
                elif t % 2:
                    ins.then_inc(h_scaled, 1)
                else:
                    step(ins, wait=False)

            def shift_tile(k, i):
                t = TILE_ORDER[norm_tiles[k]][i]
                if k < 4 and t % 2 == 0:
                    step.sync()
                    drained(dve, "row", k, "shift", t // 2, 1)
                    dve.tensor_tensor(H[:, t, :], H[:, t, :], SHIFT[:, t // 2, :], ALU.add).then_inc(h_ready[0], 1)

            def norm_tile(k, i):
                scale_tile(k, i)
                shift_tile(k, i)

            def norm(k):
                for i in range(norm_tiles[k]):
                    norm_tile(k, i)

            def norm_of_blocks(l):
                T = tiles_of[l]
                dve.wait_ge(squares, (0, 16)[l] + 4 * T)
                dve.tensor_reduce(sumsq[:, 1 + 2 * l, 0:T], sumsq_parts[:, l, 0:T, :], AX.X, ALU.add).then_inc(sums_ready, 1)
                norm(1 + 2 * l)

            def transposed(k):
                for t in TILE_ORDER[norm_tiles[k]]:
                    bank = full(dve, "hT", k, t, 0)
                    done(dve.tensor_copy(hT[:, 0:4, P * t:P * (t + 1)], bank.rearrange("p (j t) -> p j t", j=4)))

            def gated_output(l):
                for b in range(4):
                    for tp in range(tiles_of[l] // 2):
                        i = b * (tiles_of[l] // 2) + tp
                        bank = full(dve, "out", l, b, tp)
                        drained(dve, "row", 2 * l, "gate", CONTEXT if l == 0 else LATENT, 1)
                        if i >= 2:
                            dve.wait_ge(x_updated, (0, xu_moe[0])[l] + i - 1)
                        g = G[:, tp, BLK * b:BLK * (b + 1)].unsqueeze(1).broadcast_to([P, 2, BLK])
                        done(dve.tensor_tensor(PR[:, i % 2, :].rearrange("p (t n) -> p t n", t=2),
                                               bank.rearrange("p (t n) -> p t n", t=2), g, ALU.mult))

            def first_of(value, best, hot, T):
                c = cand[:, 0:T, :]
                step(dve.tensor_tensor(c, value[:, 0:T, :], best[:, 0:T].unsqueeze(2).broadcast_to([P, T, EXPERTS]), ALU.is_equal))
                step(dve.scalar_tensor_tensor(out=c, in0=c, scalar=-100.0, in1=iota[:, 0:EXPERTS].unsqueeze(1).broadcast_to([P, T, EXPERTS]),
                                              op0=ALU.mult, op1=ALU.add))
                step(dve.tensor_reduce(least[:, 0:T], c, AX.X, ALU.min))
                step(dve.tensor_tensor(hot[:, 0:T, :], c, least[:, 0:T].unsqueeze(2).broadcast_to([P, T, EXPERTS]), ALU.is_equal))

            def route(l):
                T = tiles_of[l]
                lg = logits[:, 0:T, :]
                bank = full(dve, "logit", l)
                dve.wait_ge(ld_router, 96 * (l + 1))
                done(dve.tensor_tensor(lg, bank[:, 0:36 * T].rearrange("p (t n) -> p t n", t=T),
                                       RB[:, :].unsqueeze(1).broadcast_to([P, T, GROUPS + EXPERTS]), ALU.add))
                drained(dve, "logit", l)
                g = lg[:, :, 0:GROUPS]
                step(dve.tensor_reduce(gmax[:, 0:T], g, AX.X, ALU.max))
                if T < 4:
                    step(dve.memset(rarg[:, :, :], 0.0))
                step(dve.tensor_tensor(rarg[:, 0:T, :], g, gmax[:, 0:T].unsqueeze(2).broadcast_to([P, T, GROUPS]), ALU.subtract))
                gc, gh, gp = gcand[:, 0:T, :], ghot[:, 0:T, :], gpen[:, 0:T, :]
                step(dve.tensor_scalar(gc, rarg[:, 0:T, :], 0.0, None, ALU.is_ge))
                step(dve.scalar_tensor_tensor(out=gc, in0=gc, scalar=-100.0,
                                              in1=iota[:, 0:GROUPS].unsqueeze(1).broadcast_to([P, T, GROUPS]),
                                              op0=ALU.mult, op1=ALU.add))
                step(dve.tensor_reduce(least[:, 0:T], gc, AX.X, ALU.min))
                step(dve.tensor_tensor(gh, gc, least[:, 0:T].unsqueeze(2).broadcast_to([P, T, GROUPS]), ALU.is_equal))
                step(dve.tensor_scalar(gp, gh, -NEG, NEG, ALU.mult, ALU.add))
                m = masked[:, 0:T, :].rearrange("p t (g e) -> p t g e", g=GROUPS)
                by_group = [P, T, GROUPS, PER_GROUP]
                step(dve.tensor_tensor(m, lg[:, :, GROUPS:].rearrange("p t (g e) -> p t g e", g=GROUPS),
                                       gh.unsqueeze(3).broadcast_to(by_group), ALU.mult))
                step(dve.tensor_tensor(m, m, gp.unsqueeze(3).broadcast_to(by_group), ALU.add))
                step(dve.tensor_reduce(emax[:, 0:T], masked[:, 0:T, :], AX.X, ALU.max))
                first_of(masked, emax, first_choice, T)
                step(dve.scalar_tensor_tensor(out=masked[:, 0:T, :], in0=first_choice[:, 0:T, :], scalar=NEG,
                                              in1=masked[:, 0:T, :], op0=ALU.mult, op1=ALU.add))
                step(dve.tensor_reduce(emax2[:, 0:T], masked[:, 0:T, :], AX.X, ALU.max))
                first_of(masked, emax2, second_choice, T)
                dve.tensor_tensor(chosen[:, 0:T, :], first_choice[:, 0:T, :], second_choice[:, 0:T, :],
                                  ALU.add).then_inc(one_hot, 1)
                dve.tensor_tensor(rarg[:, 4, 0:T], emax2[:, 0:T], emax[:, 0:T], ALU.subtract).then_inc(router_max, 1)
                if l == 0:
                    modulation(1, 5)
                for k in (0, 1):
                    step(dve.tensor_tensor(rows_of[:, k * T:(k + 1) * T, :, :],
                                           choices[:, k, 0:T, :].unsqueeze(2).broadcast_to([P, T, 2, EXPERTS]),
                                           const[:, C_VAL + 8 * k:C_VAL + 8 * k + 2 * T].rearrange("p (t v) -> p t v", v=2)
                                           .unsqueeze(3).broadcast_to([P, T, 2, EXPERTS]), ALU.mult), wait=False)
                bank = full(dve, "rank", l)
                step(dve.tensor_tensor(ranked[:, :, 0:T, :], choices[:, :, 0:T, :],
                                       bank[:, 0:EXPERTS * T].rearrange("p (t e) -> p t e", t=T).unsqueeze(1)
                                       .broadcast_to([P, 2, T, EXPERTS]), ALU.mult), wait=False)
                done(dve.tensor_copy(count[0:1, :], bank[0:1, EXPERTS * 4:EXPERTS * 5]))
                step.sync()
                step(dve.tensor_reduce(rank_of[:, 0:2 * T].rearrange("p (k t) -> p k t", k=2), ranked[:, :, 0:T, :], AX.X, ALU.add))

                n_blocks = T * P // CAP
                before = (0, NBLK)[l]

                def hot(b):
                    dve.scalar_tensor_tensor(
                        out=at_slot[:, b % 2, 0:2 * T, :],
                        in0=rank_of[:, 0:2 * T].unsqueeze(2).broadcast_to([P, 2 * T, CAP]), scalar=float(-CAP * b),
                        in1=iota.unsqueeze(1).broadcast_to([P, 2 * T, CAP]), op0=ALU.add,
                        op1=ALU.is_equal).then_inc(slot_hot, 1)

                hot(0)
                hot(1)
                bank = full(dve, "slots", l, 0)
                done(dve.tensor_scalar(idx[:, 0, :, :].rearrange("p v e -> p (v e)"), bank[:, 0:2 * EXPERTS],
                                       const[:, C_OFF:C_OFF + 1], None, ALU.add))
                for b in range(2, n_blocks):
                    if b >= 3:
                        dve.wait_ge(slot_used, (0, NBLK - 2)[l] + b - 2)
                    hot(b)
                dve.wait_ge(router_exp, l + 1)
                step(dve.tensor_reduce(gsum[:, 0:T], rexp[:, 0:T, :], AX.X, ALU.add))
                step(dve.scalar_tensor_tensor(out=gsum[:, 0:T], in0=rexp[:, 4, 0:T], scalar=1.0, in1=gsum[:, 0:T],
                                              op0=ALU.add, op1=ALU.mult))
                step(dve.reciprocal(topw[:, 0:T, 0], gsum[:, 0:T]))
                step(dve.tensor_tensor(topw[:, 0:T, 1], rexp[:, 4, 0:T], topw[:, 0:T, 0], ALU.mult))
                drained(dve, "rank", l)
                step(dve.tensor_scalar(blocks[0:1, :], count[0:1, :], float(CAP), None, ALU.is_gt))
                for b in range(2, n_blocks):
                    step(dve.scalar_tensor_tensor(out=blocks[0:1, :], in0=count[0:1, :], scalar=float(CAP * b),
                                                  in1=blocks[0:1, :], op0=ALU.is_gt, op1=ALU.add))
                step(dve.tensor_tensor(packed[0:1, :], blocks[0:1, :], const[0:1, C_POW:C_POW + EXPERTS], ALU.mult))
                step(dve.tensor_reduce(words[0:1, :], packed[0:1, :].rearrange("p (w e) -> p w e", e=PER_LOOP), AX.X, ALU.add))
                bank = full(dve, "slots", l, 1)
                done(dve.tensor_scalar(idx[:, 1:n_blocks, :, :].rearrange("p b v e -> p (b v e)"),
                                       bank[:, 0:2 * EXPERTS * (n_blocks - 1)],
                                       const[:, C_OFF:C_OFF + 1], None, ALU.add))
                drained(dve, "slots", l, 1)
                dve.tensor_copy(extra_i[0:1, l, :], words[0:1, :]).then_inc(extra_ready, 1)

            extras = dve.alloc_register("dve_extras")
            dve.reg_mov(extras, 0)

            def experts(l):
                n0 = EXPERTS * l

                def hidden(i, q):
                    n, b = i * PER_LOOP + (n0 + q), q % 2
                    dve.wait_ge(gate_ready, n + 1)
                    dve.tensor_tensor(HID[:, b, :], SA[:, b, :], ps[CAP:P, 2 + b, 0:BLK], ALU.mult).then_inc(hid_ready, 1)

                def copy_hT(i, q):
                    n, b = i * PER_LOOP + (n0 + q), q % 2
                    dve.wait_ge(hidT_full, n + 1)
                    dve.tensor_copy(HT[:, b, :, :].rearrange("p f s -> p (f s)"),
                                    ps[:, 4, P * b:P * (b + 1)]).then_inc(hidT_ready, 1)

                def more(q, count):
                    bank = ps[:, 7, :]
                    with dve.If(count > 0):
                        with dve.Fori(0, count):
                            dve.reg_add(extras, extras, 1)
                            x = dve.snap(extras)
                            dve.wait_ge(x_gate_ready, x)
                            dve.tensor_tensor(HIDX, SAX, bank[CAP:P, 0:BLK], ALU.mult).then_inc(x_hid_ready, 1)
                            dve.wait_ge(x_hidT_full, x)
                            dve.tensor_copy(HTX.rearrange("p f s -> p (f s)"), bank[:, 0:P]).then_inc(x_hidT_ready, 1)

                def one(i, q, count, ahead=True):
                    copy_hT(i, q)
                    if ahead:
                        hidden(*job_after(i, q, 1))
                    more(q, count)

                hidden(0, 0)
                dve.wait_ge(extra_ready, l + 1)
                last = EXPERTS // PER_LOOP - 1
                with dve.Fori(0, last) as i:
                    c = extra_counts(dve, l, i)
                    for q in range(PER_LOOP):
                        one(i, q, c[q])
                c = extra_counts(dve, l, last)
                for q in range(PER_LOOP):
                    one(last, q, c[q], ahead=(q < 3))

            def combine_and_norm(l):
                T = tiles_of[l]

                def combine_tile(i):
                    t = TILE_ORDER[T][i]
                    first, total, y = back[t]
                    a, b = y[:, D * first:D * (first + 1)], y[:, D * total:D * (total + 1)]
                    dve.wait_ge(y_scaled, (0, 4)[l] + i + 1)
                    step(dve.scalar_tensor_tensor(out=b, in0=b, scalar=topw[:, t, total:total + 1], in1=a,
                                                  op0=ALU.mult, op1=ALU.add))
                    dve.tensor_tensor(b, b, G[:, t // 2, :], ALU.mult).then_inc(combined, 1)

                for i in range(T):
                    combine_tile(i)
                    if i >= 2:
                        norm_tile(2 * l + 2, i - 2)
                for i in range(T - 2, T):
                    norm_tile(2 * l + 2, i)

            modulation(0, 1)
            scale_rows(0)
            for i in range(4):
                scale_tile(0, i)
            modulation(0, 0)
            for i in range(4):
                shift_tile(0, i)
            transposed(0)

            def tap(ct, k):
                out = Y[:, ct, :].rearrange("p (s t) -> p s t", s=2)
                z = Z[:, ct, :, k:k + SEQ]
                if k == 0:
                    return dve.tensor_scalar(out, z, chan[:, ct, 0:1], chan[:, ct, TAPS:TAPS + 1], ALU.mult, ALU.add)
                return dve.scalar_tensor_tensor(out=out, in0=z, scalar=chan[:, ct, k:k + 1], in1=out,
                                                op0=ALU.mult, op1=ALU.add)

            for pair in (0, 1):
                dve.wait_ge(gated_in, 2 * pair + 2)
                for k in range(TAPS):
                    for i in (0, 1):
                        if k:
                            dve.wait_ge(conv_step, 2 * (TAPS * pair + k - 1) + i + 1)
                        tap(2 * pair + i, k).then_inc(conv_step, 1)

            def maxima(n):
                bank = full(dve, "S", n)
                if n >= 1:
                    dve.wait_ge(max_ready, n)
                step(dve.tensor_reduce(m1, bank[:, 0 if n % 4 < 2 else SEQ:TOK], AX.X, ALU.max))
                dve.tensor_scalar(nmax[:, n:n + 1], m1, -1.0, None, ALU.mult).then_inc(max_ready, 1)

            def normalise(n):
                drained(dve, "S", n)
                r, probs = rsum[:, 0:1], PROBS[n % S_AHEAD][:, 0 if n % 4 < 2 else SEQ:TOK]
                if n >= 1:
                    dve.wait_ge(probs_ready, n)
                step(dve.reciprocal(r, sums[:, n % 4:n % 4 + 1]))
                dve.tensor_scalar(probs, probs, r, None, ALU.mult).then_inc(probs_ready, 1)

            units = 4 * A_HEADS
            for n in range(S_AHEAD):
                maxima(n)
            normalise(0)
            for n in range(units):
                if n + 1 < units:
                    normalise(n + 1)
                if n + S_AHEAD < units:
                    maxima(n + S_AHEAD)
                if n in MOD_AFTER:
                    modulation(*MOD_AFTER[n])
            bank = full(dve, "mean")
            for ct in range(4):
                ins = dve.scalar_tensor_tensor(out=Y[:, ct, :], in0=bank, scalar=-1.0 / 512, in1=Y[:, ct, :],
                                               op0=ALU.mult, op1=ALU.add)
                ins.then_inc(centred, 1)
            done(dve.tensor_copy(m1, bank[:, 0:1]))
            modulation(1, 2)
            drained(dve, "var")
            step(dve.reciprocal(SD, SD))
            for ct in range(4):
                dve.tensor_tensor(Y[:, ct, :], Y[:, ct, :], SD, ALU.mult).then_inc(ln_scaled, 1)
            dve.wait_ge(ln_scaled, 4)
            gated_output(0)
            scale_rows(1)
            norm_of_blocks(0)
            modulation(1, 3)
            modulation(1, 4)
            transposed(1)
            route(0)
            dve.wait_ge(ld_lam, 32)
            for i in (0, 1):
                step(dve.tensor_tensor_reduce(PR[:, 1, 64 * i:64 * i + 64], LAMROW[:, 128 * i:128 * i + 64],
                                              LAMROW[:, 128 * i + 64:128 * i + 128], 1.0, 0.0, ALU.mult, ALU.add,
                                              lam[:, i:i + 1]), wait=False)
            dve.tensor_scalar(sublns, subln, 1.0 - LAM_INIT, None, ALU.mult).then_inc(lam_sums, 1)
            experts(0)

            scale_rows(2)
            combine_and_norm(0)
            transposed(2)
            dve.wait_ge(lam_exp, 1)
            step(dve.tensor_tensor(lam[:, 4:5], lam[:, 3:4], lam[:, 2:3], ALU.subtract))
            step(dve.tensor_scalar(lam[:, 5:6], lam[:, 4:5], -LAM_INIT, None, ALU.add))
            for col in (0, SEQ + 1):
                step(dve.memset(CU[:, :, col:col + 1], 0.0))
            dve.wait_ge(ld_rot, 16)
            def diff_maxima(n):
                banks = [full(dve, "DS", n, m) for m in (0, 1)]
                for m in (0, 1):
                    step(dve.tensor_reduce((m1, m2)[m], banks[m], AX.X, ALU.max), wait=False)
                step.sync()
                dve.tensor_scalar(nmax[:, 2 * n:2 * n + 2], small[:, 96:98], -1.0, None, ALU.mult).then_inc(max_ready, 1)
                dve.wait_ge(max_ready, units + n + 1)

            def diff_normalise(n):
                drained(dve, "DS", n, 1)
                if n >= 1:
                    dve.wait_ge(probs_ready, units + n)
                k, first, second = 2 * (n % 4), DP[:, 2 * (n % 2), :], DP[:, 2 * (n % 2) + 1, :]
                step(dve.reciprocal(rsum[:, 0:2], sums[:, k:k + 2]))
                step(dve.tensor_tensor(rsum[:, 2:3], rsum[:, 1:2], lam[:, 5:6], ALU.mult), wait=False)
                step(dve.tensor_scalar(first, first, rsum[:, 0:1], None, ALU.mult))
                dve.scalar_tensor_tensor(out=first, in0=second, scalar=rsum[:, 2:3], in1=first,
                                         op0=ALU.mult, op1=ALU.add).then_inc(probs_ready, 1)

            tile = 0
            for what, b, _ in ODD_BLOCKS:
                if (what, b) == ("cc", 0):
                    diff_maxima(0)
                    diff_maxima(1)
                if what in ("dq", "dk"):
                    for f in (0, 1):
                        x = (DQ if what == "dq" else DK)[:, 2 * b + f, 0:SEQ]
                        r = ROT[:, tile % 2, 0:SEQ]
                        bank = full(dve, what + "swap", b, f)
                        if tile >= 2:
                            dve.wait_ge(rot_ready, tile - 1)
                        done(dve.tensor_tensor(r, bank[:, 0:SEQ], SIN, ALU.mult))
                        step(dve.tensor_tensor(x, x, COS, ALU.mult))
                        drained(dve, what + "swap", b, f)
                        dve.tensor_tensor(x, x, r, ALU.add).then_inc(rot_ready, 1)
                        tile += 1
                elif what == "cu":
                    drained(dve, "cc", b)
                    done(dve.tensor_tensor(CU[:, 2 * b:2 * b + 2, 1:1 + SEQ],
                                           full(dve, "cu", b).rearrange("p (c t) -> p c t", c=2),
                                           CC[:, 2 * b:2 * b + 2, :], ALU.mult))
                    drained(dve, "cu", b)
                    for k in range(3):
                        for ct in (2 * b, 2 * b + 1):
                            z, w = CU[:, ct, k:k + SEQ], chan[:, ct, 34 + k:35 + k]
                            if k == 0:
                                step(dve.tensor_scalar(CV[:, ct, :], z, w, None, ALU.mult), wait=False)
                            else:
                                step(dve.scalar_tensor_tensor(out=CV[:, ct, :], in0=z, scalar=w, in1=CV[:, ct, :],
                                                              op0=ALU.mult, op1=ALU.add), wait=False)
                        step.sync()
                elif what == "cb":
                    cv = CV[:, 2 * b:2 * b + 2, :]
                    done(dve.tensor_tensor(cv, full(dve, "cb", b).rearrange("p (c t) -> p c t", c=2), cv, ALU.mult))

            def diff_output(n):
                done(dve.tensor_copy(OD[:, n, :], full(dve, "DO", n)[:, 0:P]))
                drained(dve, "DO", n)
                scratch = RM[:, P * n:P * (n + 1)]
                dve.tensor_tensor_reduce(scratch, OD[:, n, :], OD[:, n, :], 1.0, 0.0, ALU.mult, ALU.add,
                                         dss[:, n:n + 1]).then_inc(o_squared, 1)

            diff_normalise(0)
            for n in range(2 * D_HEADS):
                if n + 1 < 2 * D_HEADS:
                    diff_normalise(n + 1)
                if n + 2 < 2 * D_HEADS:
                    diff_maxima(n + 2)
                if n >= 1:
                    diff_output(n - 1)
            diff_output(2 * D_HEADS - 1)
            dve.wait_ge(o_root, 1)
            step(dve.reciprocal(drstd, droot))
            for n in range(2 * D_HEADS):
                dve.tensor_scalar(OD[:, n, :], OD[:, n, :], drstd[:, n:n + 1], None, ALU.mult).then_inc(o_scaled, 1)
            gated_output(1)
            scale_rows(3, (LATENT,))
            norm_of_blocks(1)
            transposed(3)
            route(1)
            experts(1)
            combine_and_norm(1)

        @block.gpsimd
        def _(pool):
            step = chained(pool, pool_step)
            step(pool.memset(modrow[:, :, :], 0.0), wait=False)
            pool.memset(grow[:, :, :], 0.0).then_inc(zeroed, 1)
            pool.memset(RM[:, :], 0.0).then_inc(z_clear, 1)

            def norm_tile(k, i):
                t = TILE_ORDER[norm_tiles[k]][i]
                pool.wait_ge(h_scaled, (h_before[k] + i) // 2 + 1)
                drained(pool, "row", k, "shift", t // 2, 1)
                pool.tensor_tensor(H[:, t, :], H[:, t, :], SHIFT[:, t // 2, :], ALU.add).then_inc(h_ready[1], 1)

            def norm(k):
                for i in range(0, norm_tiles[k], 2):
                    norm_tile(k, i)

            def mask(h):
                pool.wait_ge(ld_bias[h % 4], 32 * (h // 4 + 1))
                for half in (0, 1):
                    b = BIAS[64 * half:64 * half + 64, h % 4, :, :]
                    lo, hi = b[:, :, 0:48], b[:, :, 16:64]
                    step(pool.affine_select(out=lo, in_=lo, compare_op=ALU.is_ge, fill=NEG, base=-55,
                                            pattern=[[0, 6], [1, 48]], channel_multiplier=1))
                    ins = pool.affine_select(out=hi, in_=hi, compare_op=ALU.is_ge, fill=NEG, base=54,
                                             pattern=[[0, 6], [-1, 48]], channel_multiplier=-1)
                    if half == 0:
                        step(ins)
                    else:
                        ins.then_inc(bias_ready, 1)
                pool.wait_ge(bias_ready, h + 1)

            def add_outputs(l):
                for b in range(4):
                    for tp in range(tiles_of[l] // 2):
                        i = b * (tiles_of[l] // 2) + tp
                        drained(pool, "out", l, b, tp)
                        x = X[:, 2 * tp:2 * tp + 2, BLK * b:BLK * (b + 1)]
                        pool.tensor_tensor(x, x, PR[:, i % 2, :].rearrange("p (t n) -> p t n", t=2),
                                           ALU.add).then_inc(x_updated, 1)

            extras = pool.alloc_register("pool_extras")
            pool.reg_mov(extras, 0)

            def experts(l):
                n0 = EXPERTS * l
                pool.wait_ge(h_stored, 16 * (4 if l == 0 else 6))
                full(pool, "hT", 1 + 2 * l, TILE_ORDER[tiles_of[l]][-1], 1)
                step(pool.memset(XG.rearrange("p b d -> p (b d)"), 0.0), wait=False)
                step(pool.memset(XGX, 0.0))
                drained(pool, "slots", l, 0)

                def gather(i, q):
                    n = i * PER_LOOP + (n0 + q)
                    if not (isinstance(i, int) and i == 0):
                        pool.wait_ge(xT_full, n - 3)
                    e = i * PER_LOOP + q
                    col = idx[:, 0, 0, e:e + 1] if isinstance(e, int) else idx[:, 0, 0, bass.ds(e, 1)]
                    pool.tensor_copy(GIDX[q % 4], col).then_inc(gidx_ready, 1)
                    pool.wait_ge(gidx_ready, n + 1)
                    pool.sem_inc(pool_passed, 1)
                    pool.indirect_dma_start(out=XG[:, q % 4, :], out_offset=None, in_=hrow[l],
                                            in_offset=bass.IndirectOffsetOnAxis(ap=GIDX[q % 4], axis=0),
                                            bounds_check=2 * tokens[l] - 1, oob_is_err=False).then_inc(gathered[q % 4], 16)

                def scatter(i, q):
                    n, b = i * PER_LOOP + (n0 + q), q % 2
                    pool.wait_ge(y_ready, n + 1)
                    e = i * PER_LOOP + q
                    col = idx[:, 0, 1, e:e + 1] if isinstance(e, int) else idx[:, 0, 1, bass.ds(e, 1)]
                    pool.tensor_copy(SIDX[b], col).then_inc(sidx_ready, 1)
                    pool.wait_ge(sidx_ready, n + 1)
                    pool.sem_inc(pool_passed, 1)
                    pool.indirect_dma_start(out=pair_out[l], out_offset=bass.IndirectOffsetOnAxis(ap=SIDX[b], axis=0),
                                            in_=YS[:, b, :], in_offset=None, bounds_check=4 * tokens[l] - 1,
                                            oob_is_err=False).then_inc(scattered[b], 16)

                def stored(x):
                    with pool.If(x > 0):
                        pool.wait_ge(x_scattered, x * 16)

                def fetch(e, k):
                    x = pool.snap(extras)
                    stored(x)
                    for v, dst in ((0, GIDXX), (1, SIDXX)):
                        pool.tensor_copy(dst, idx[:, bass.ds(k + 1, 1), v, bass.ds(e, 1)]
                                         .rearrange("p b e -> p (b e)")).then_inc(x_gidx, 1)
                    pool.wait_ge(x_gidx, x * 2 + 2)
                    pool.sem_inc(pool_passed, 1)
                    pool.indirect_dma_start(out=XGX, out_offset=None, in_=hrow[l],
                                            in_offset=bass.IndirectOffsetOnAxis(ap=GIDXX, axis=0),
                                            bounds_check=2 * tokens[l] - 1, oob_is_err=False).then_inc(x_gathered, 16)

                def finish():
                    pool.reg_add(extras, extras, 1)
                    x = pool.snap(extras)
                    pool.wait_ge(x_y_ready, x)
                    pool.sem_inc(pool_passed, 1)
                    pool.indirect_dma_start(out=pair_out[l],
                                            out_offset=bass.IndirectOffsetOnAxis(ap=SIDXX, axis=0),
                                            in_=YSX, in_offset=None, bounds_check=4 * tokens[l] - 1,
                                            oob_is_err=False).then_inc(x_scattered, 16)

                def ahead(i, q, count):
                    with pool.If(count > 0):
                        fetch(i * PER_LOOP + q, 0)

                def more(i, q, count):
                    with pool.If(count > 0):
                        with pool.If(count > 1):
                            with pool.Fori(0, count - 1) as k:
                                finish()
                                fetch(i * PER_LOOP + q, k + 1)
                        finish()

                def one(i, q, counts, last=False):
                    if not last:
                        gather(i + 1, q)
                    more(i, q, counts[q])
                    if q + 1 < PER_LOOP:
                        ahead(i, q + 1, counts[q + 1])
                    elif not last:
                        ahead(i + 1, 0, extra_counts(pool, l, i + 1)[0])
                    scatter(i, q)

                for q in range(PER_LOOP):
                    gather(0, q)
                pool.wait_ge(extra_ready, l + 1)
                ahead(0, 0, extra_counts(pool, l, 0)[0])
                last = EXPERTS // PER_LOOP - 1
                with pool.Fori(0, last) as i:
                    counts = extra_counts(pool, l, i)
                    for q in range(PER_LOOP):
                        one(i, q, counts)
                counts = extra_counts(pool, l, last)
                for q in range(PER_LOOP):
                    one(last, q, counts, last=True)
                for b in (0, 1):
                    pool.wait_ge(scattered[b], 16 * (n0 + EXPERTS) // 2)
                stored(pool.snap(extras))

            def combine_and_norm(l):
                T = tiles_of[l]
                pool.sem_inc(pairs_stored, 1)
                for i, t in enumerate(TILE_ORDER[T]):
                    _, total, y = back[t]
                    pool.wait_ge(combined, (0, 4)[l] + i + 1)
                    pool.tensor_tensor(X[:, t, :], X[:, t, :], y[:, D * total:D * (total + 1)], ALU.add).then_inc(x_updated, 1)
                    if i == 2:
                        norm_tile(2 * l + 2, 0)
                if T == 4:
                    norm_tile(2 * l + 2, 2)

            norm(0)
            for h in range(4):
                mask(h)
            for b in (0, 1):
                for f in (0, 1):
                    ct = 2 * b + f
                    drained(pool, "g", b, f)
                    z = Z[:, ct, :, PAD:PAD + SEQ]
                    pool.tensor_tensor(z, z, SG[:, ct % 2, :].rearrange("p (s t) -> p s t", s=2), ALU.mult).then_inc(gated_in, 1)
            for h in range(4, A_HEADS):
                mask(h)
            add_outputs(0)
            norm(1)
            experts(0)
            combine_and_norm(0)

            add_outputs(1)
            norm(3)
            experts(1)
            combine_and_norm(1)


_INS = ["x", "c", "ctx", "c_ctx", "w_mod", "b_mod", "norm_mix", "norm_ffn", "norm_final",
        "even_w_in", "even_w_out", "even_rpb", "even_dw", "even_dw_b", "even_ln_g", "even_ln_b",
        "odd_w_in", "odd_w_out", "odd_conv", "odd_lambda", "odd_subln",
        "moe_wg", "moe_bg", "moe_we", "moe_be", "moe_w1", "moe_w3", "moe_w2"]


def kernel(**inputs):
    import concourse.bacc as _bacc
    from concourse.bass_utils import run_bass_kernel_spmd as _run

    nc = _bacc.Bacc("TRN2", target_bir_lowering=False, num_devices=1)
    consts, rotary = constants()
    arrays, aps = {}, {}
    for name, a in [(n, inputs[n]) for n in _INS] + [("consts", consts), ("rotary", rotary)]:
        a = np.ascontiguousarray(a)
        arrays[f"in_{name}"] = a
        aps[name] = nc.dram_tensor(f"in_{name}", a.shape, mybir.dt.from_np(a.dtype), kind="ExternalInput").ap()
    aps["out"] = nc.dram_tensor("out_x", (1, SEQ, D), F32, kind="ExternalOutput").ap()
    trunk(nc, aps)
    r = _run(nc, [arrays], core_ids=[0])
    return r.results[0]["out_x"]
```
